# Optimizing a Trainium2 kernel written in Bass

```python
import math
import jax, jax.numpy as jnp
from jax import lax
import numpy as np

D_MODEL = 1024
BATCH = 1
SEQ = 1024
DEPTH = 1

N_META = 16
ATTN_WIDTH = D_MODEL // 2
SSM_WIDTH = D_MODEL - ATTN_WIDTH
N_ATTN_HEADS = 4
QK_DIM = ATTN_WIDTH // N_ATTN_HEADS // 2
V_DIM = 2 * QK_DIM
ROT_DIM = QK_DIM // 4
ROPE_THETA = 500000.0
SSM_GROUP = 16
N_SSM_GROUPS = SSM_WIDTH // SSM_GROUP
SSM_STATE = 64
D_FF = -(-8 * D_MODEL // (3 * 256)) * 256
Q_BLOCK = 128
EPS = 1e-6
QK_COLS = N_ATTN_HEADS * QK_DIM
V_COLS = N_ATTN_HEADS * V_DIM
IN_COLS = 4 * QK_COLS + V_COLS + SSM_WIDTH


def rms_norm(x, g):
    x32 = x.astype(jnp.float32)
    y = x32 * lax.rsqrt(jnp.mean(x32 * x32, axis=-1, keepdims=True) + EPS)
    return (y * g.astype(jnp.float32)).astype(x.dtype)

def lambda_init(layer_idx):
    return 0.8 - 0.6 * math.exp(-0.3 * layer_idx)

def rope_tables(length):
    pos = jnp.arange(length, dtype=jnp.float32)
    inv_freq = ROPE_THETA ** (-jnp.arange(0, ROT_DIM, 2, dtype=jnp.float32) / ROT_DIM)
    ang = pos[:, None] * inv_freq[None, :]
    ang = jnp.concatenate([ang, ang], axis=-1)
    return jnp.cos(ang), jnp.sin(ang)

def partial_rope(t, cos, sin):
    t_rot, t_pass = t[..., :ROT_DIM], t[..., ROT_DIM:]
    half = ROT_DIM // 2
    rot_half = jnp.concatenate([-t_rot[..., half:], t_rot[..., :half]], axis=-1)
    t_rot = (t_rot * cos + rot_half * sin).astype(t.dtype)
    return jnp.concatenate([t_rot, t_pass], axis=-1)

def diff_attention(q1, q2, k1, k2, v, lam):
    b, h, lp, d = q1.shape
    nb = lp // Q_BLOCK
    scale = 1.0 / math.sqrt(d)
    k_pos = jnp.arange(lp)
    v32 = v.astype(jnp.float32)

    def to_blocks(t):
        return t.reshape(b, h, nb, Q_BLOCK, t.shape[-1]).transpose(2, 0, 1, 3, 4)

    def block(args):
        q1b, q2b, start = args
        q_pos = start + jnp.arange(Q_BLOCK)
        causal = k_pos[None, :] <= q_pos[:, None]

        def probs(qb, k):
            s = jnp.einsum('bhqd,bhkd->bhqk', qb, k, preferred_element_type=jnp.float32) * scale
            return jax.nn.softmax(jnp.where(causal, s, -jnp.inf), axis=-1)

        attn = probs(q1b, k1) - lam * probs(q2b, k2)
        return jnp.einsum('bhqk,bhkd->bhqd', attn, v32)

    starts = jnp.arange(nb, dtype=jnp.int32) * Q_BLOCK
    out = lax.map(block, (to_blocks(q1), to_blocks(q2), starts))
    return out.transpose(1, 2, 0, 3, 4).reshape(b, h, lp, v.shape[-1])

def s5_ssm(u, a_re, a_im, log_dt, b_re, b_im, c_re, c_im, d_skip):
    u = u.astype(jnp.float32)
    dt = jnp.exp(log_dt.astype(jnp.float32))[:, None]
    a_re = a_re.astype(jnp.float32)
    a_im = a_im.astype(jnp.float32)
    mag = jnp.exp(a_re * dt)
    ang = a_im * dt
    ab_re, ab_im = mag * jnp.cos(ang), mag * jnp.sin(ang)
    den = a_re * a_re + a_im * a_im
    nr, ni = ab_re - 1.0, ab_im
    f_re = (nr * a_re + ni * a_im) / den
    f_im = (ni * a_re - nr * a_im) / den
    b_re = b_re.astype(jnp.float32)
    b_im = b_im.astype(jnp.float32)
    bb_re = f_re[..., None] * b_re - f_im[..., None] * b_im
    bb_im = f_re[..., None] * b_im + f_im[..., None] * b_re
    bu_re = jnp.einsum('blgh,gph->blgp', u, bb_re)
    bu_im = jnp.einsum('blgh,gph->blgp', u, bb_im)
    ar = jnp.broadcast_to(ab_re, bu_re.shape)
    ai = jnp.broadcast_to(ab_im, bu_re.shape)

    def combine(e1, e2):
        ar1, ai1, br1, bi1 = e1
        ar2, ai2, br2, bi2 = e2
        return (ar2 * ar1 - ai2 * ai1,
                ar2 * ai1 + ai2 * ar1,
                ar2 * br1 - ai2 * bi1 + br2,
                ar2 * bi1 + ai2 * br1 + bi2)

    _, _, x_re, x_im = lax.associative_scan(combine, (ar, ai, bu_re, bu_im), axis=1)
    y = (jnp.einsum('blgp,ghp->blgh', x_re, c_re.astype(jnp.float32))
         - jnp.einsum('blgp,ghp->blgh', x_im, c_im.astype(jnp.float32)))
    y = y + d_skip.astype(jnp.float32).reshape(N_SSM_GROUPS, SSM_GROUP) * u
    bsz, length = u.shape[0], u.shape[1]
    return y.reshape(bsz, length, N_SSM_GROUPS * SSM_GROUP)

def first_inputs(seed: int = 0) -> dict:
    key = jax.random.key(seed)
    ks = jax.random.split(key, 32)
    f32 = jnp.float32

    def nrm(k, shape, scale):
        return jax.random.normal(k, shape, f32) * scale

    def gain(k, shape):
        return 1.0 + 0.02 * jax.random.normal(k, shape, f32)

    n_idx = jnp.arange(SSM_STATE, dtype=f32)
    a_re = -0.5 + 0.01 * jax.random.normal(ks[8], (DEPTH, N_SSM_GROUPS, SSM_STATE), f32)
    a_im = math.pi * n_idx[None, None, :] + 0.01 * jax.random.normal(ks[9], (DEPTH, N_SSM_GROUPS, SSM_STATE), f32)
    log_dt = jax.random.uniform(ks[10], (DEPTH, N_SSM_GROUPS), f32, math.log(1e-3), math.log(1e-1))
    return {
        "x": nrm(ks[0], (BATCH, SEQ, D_MODEL), 1.0),
        "meta": nrm(ks[1], (N_META, D_MODEL), 1.0),
        "pre_mix_g": gain(ks[2], (DEPTH, D_MODEL)),
        "w_in": nrm(ks[3], (DEPTH, D_MODEL, IN_COLS), D_MODEL ** -0.5),
        "lambda_q1": nrm(ks[4], (DEPTH, QK_DIM), 0.1),
        "lambda_k1": nrm(ks[5], (DEPTH, QK_DIM), 0.1),
        "lambda_q2": nrm(ks[6], (DEPTH, QK_DIM), 0.1),
        "lambda_k2": nrm(ks[7], (DEPTH, QK_DIM), 0.1),
        "subln_g": gain(ks[11], (DEPTH, V_DIM)),
        "a_re": a_re,
        "a_im": a_im,
        "log_dt": log_dt,
        "b_re": nrm(ks[12], (DEPTH, N_SSM_GROUPS, SSM_STATE, SSM_GROUP), (2.0 * SSM_GROUP) ** -0.5),
        "b_im": nrm(ks[13], (DEPTH, N_SSM_GROUPS, SSM_STATE, SSM_GROUP), (2.0 * SSM_GROUP) ** -0.5),
        "c_re": nrm(ks[14], (DEPTH, N_SSM_GROUPS, SSM_GROUP, SSM_STATE), (2.0 * SSM_STATE) ** -0.5),
        "c_im": nrm(ks[15], (DEPTH, N_SSM_GROUPS, SSM_GROUP, SSM_STATE), (2.0 * SSM_STATE) ** -0.5),
        "d_skip": nrm(ks[16], (DEPTH, SSM_WIDTH), 1.0),
        "w_glu": nrm(ks[17], (DEPTH, SSM_WIDTH, SSM_WIDTH), SSM_WIDTH ** -0.5),
        "b_glu": nrm(ks[18], (DEPTH, SSM_WIDTH), 0.02),
        "ssm_out_g": gain(ks[19], (DEPTH, SSM_WIDTH)),
        "w_out": nrm(ks[20], (DEPTH, D_MODEL, D_MODEL), D_MODEL ** -0.5),
        "post_mix_g": gain(ks[21], (DEPTH, D_MODEL)),
        "pre_ffn_g": gain(ks[22], (DEPTH, D_MODEL)),
        "w_gate": nrm(ks[23], (DEPTH, D_MODEL, D_FF), D_MODEL ** -0.5),
        "w_up": nrm(ks[24], (DEPTH, D_MODEL, D_FF), D_MODEL ** -0.5),
        "w_down": nrm(ks[25], (DEPTH, D_FF, D_MODEL), D_FF ** -0.5),
        "post_ffn_g": gain(ks[26], (DEPTH, D_MODEL)),
    }

def first_block(x, meta, pre_mix_g, w_in, lambda_q1, lambda_k1, lambda_q2, lambda_k2, subln_g,
              a_re, a_im, log_dt, b_re, b_im, c_re, c_im, d_skip, w_glu, b_glu, ssm_out_g,
              w_out, post_mix_g, pre_ffn_g, w_gate, w_up, w_down, post_ffn_g):
    bsz = x.shape[0]
    meta_b = jnp.broadcast_to(meta.astype(x.dtype)[None], (bsz, N_META, x.shape[-1]))
    h_res = jnp.concatenate([meta_b, x], axis=1)
    length = h_res.shape[1]
    l_pad = -(-length // Q_BLOCK) * Q_BLOCK
    cos, sin = rope_tables(length)

    def heads(t, dim):
        t = t.reshape(bsz, length, N_ATTN_HEADS, dim).transpose(0, 2, 1, 3)
        return t

    def pad(t):
        return jnp.pad(t, ((0, 0), (0, 0), (0, l_pad - length), (0, 0)))

    for l in range(DEPTH):
        lam_init = lambda_init(l)
        h = rms_norm(h_res, pre_mix_g[l])
        proj = jnp.einsum('bld,dc->blc', h, w_in[l])
        q1, q2, k1, k2, v, u = jnp.split(
            proj, [QK_COLS, 2 * QK_COLS, 3 * QK_COLS, 4 * QK_COLS, 4 * QK_COLS + V_COLS], axis=-1)

        q1 = pad(partial_rope(heads(q1, QK_DIM), cos, sin))
        q2 = pad(partial_rope(heads(q2, QK_DIM), cos, sin))
        k1 = pad(partial_rope(heads(k1, QK_DIM), cos, sin))
        k2 = pad(partial_rope(heads(k2, QK_DIM), cos, sin))
        vh = pad(heads(v, V_DIM))
        lam = (jnp.exp(jnp.sum(lambda_q1[l].astype(jnp.float32) * lambda_k1[l].astype(jnp.float32)))
               - jnp.exp(jnp.sum(lambda_q2[l].astype(jnp.float32) * lambda_k2[l].astype(jnp.float32)))
               + lam_init)
        o = diff_attention(q1, q2, k1, k2, vh, lam)[:, :, :length]
        o = rms_norm(o, subln_g[l]) * (1.0 - lam_init)
        o = o.transpose(0, 2, 1, 3).reshape(bsz, length, V_COLS).astype(h.dtype)

        y = s5_ssm(u.reshape(bsz, length, N_SSM_GROUPS, SSM_GROUP), a_re[l], a_im[l], log_dt[l],
                   b_re[l], b_im[l], c_re[l], c_im[l], d_skip[l])
        y = jax.nn.gelu(y, approximate=False)
        y = y * jax.nn.sigmoid(jnp.einsum('blc,cd->bld', y, w_glu[l].astype(jnp.float32))
                               + b_glu[l].astype(jnp.float32))
        y = rms_norm(y, ssm_out_g[l]).astype(h.dtype)

        mix = jnp.einsum('blc,cd->bld', jnp.concatenate([o, y], axis=-1), w_out[l])
        h_res = h_res + rms_norm(mix, post_mix_g[l])

        h = rms_norm(h_res, pre_ffn_g[l])
        f = jax.nn.silu(jnp.einsum('bld,df->blf', h, w_gate[l])) * jnp.einsum('bld,df->blf', h, w_up[l])
        f = jnp.einsum('blf,fd->bld', f, w_down[l])
        h_res = h_res + rms_norm(f, post_ffn_g[l])

    return h_res[:, N_META:]


_first_inputs = first_inputs


def first_inputs(seed=0):
    import zlib

    import numpy as np

    out = dict(_first_inputs(seed))
    spreads = {}
    factors = {}
    for name, (base, spread) in spreads.items():
        noise = np.random.default_rng([zlib.crc32(name.encode()), seed]).standard_normal(out[name].shape)
        drawn = base * np.exp(spread * noise) if base else spread * noise
        out[name] = __import__('jax').numpy.asarray(drawn.astype(out[name].dtype))
    for name, factor in factors.items():
        out[name] = (out[name] * factor).astype(out[name].dtype)
    return out


_narrow_inputs = first_inputs


def first_inputs(seed=0):
    out = dict(_narrow_inputs(seed))
    wider = {'lambda_k1': 3.91,
     'lambda_q2': 4.15,
     'subln_g': 5.71,
     'a_re': 12.0,
     'b_glu': 12.0,
     'ssm_out_g': 5.52,
     'post_mix_g': 3.74,
     'pre_ffn_g': 3.85,
     'post_ffn_g': 5.46}
    for name, times in wider.items():
        mean = out[name].mean()
        out[name] = (mean + times * (out[name] - mean)).astype(out[name].dtype)
    return out


D_PLE = 256
RET_HEAD_DIM = 128
RET_WIDTH = D_MODEL // 2
RET_HEADS = RET_WIDTH // RET_HEAD_DIM
RET_CHUNK = 128
RWKV_HEAD_DIM = 64
RWKV_WIDTH = D_MODEL - RET_WIDTH
RWKV_HEADS = RWKV_WIDTH // RWKV_HEAD_DIM
DECAY_LORA = 64
AAA_LORA = 64
GATE_LORA = 128
D_FF_2 = ((8 * D_MODEL + 3 * 256 - 1) // (3 * 256)) * 256
RET_COLS = 4 * RET_WIDTH
RWKV_COLS = 3 * RWKV_WIDTH + DECAY_LORA + AAA_LORA + GATE_LORA
IN_COLS_2 = RET_COLS + RWKV_COLS
NORM_EPS = 1e-6
RET_GN_EPS = 1e-5
RWKV_GN_EPS = 64e-5


def rms_norm_2(x, w):
    x32 = x.astype(jnp.float32)
    y = x32 * lax.rsqrt(jnp.mean(x32 * x32, axis=-1, keepdims=True) + NORM_EPS)
    return (y * w.astype(jnp.float32)).astype(x.dtype)

def head_norm(y, eps):
    mu = jnp.mean(y, axis=-1, keepdims=True)
    var = jnp.mean(jnp.square(y - mu), axis=-1, keepdims=True)
    return (y - mu) * lax.rsqrt(var + eps)

def rotate_every_two(t):
    t1 = t[..., 0::2]
    t2 = t[..., 1::2]
    return jnp.stack((-t2, t1), axis=-1).reshape(t.shape)

def retention(q, k, v):
    B, S, H, d = q.shape
    C = RET_CHUNK
    N = S // C
    pos = jnp.arange(S, dtype=jnp.float32)
    angle = 1.0 / (10000.0 ** jnp.linspace(0.0, 1.0, d // 2, dtype=jnp.float32))
    angle = jnp.repeat(angle, 2)
    phase = pos[:, None] * angle[None, :]
    sin = jnp.sin(phase)[:, None, :]
    cos = jnp.cos(phase)[:, None, :]
    q = q * cos + rotate_every_two(q) * sin
    k = (k * cos + rotate_every_two(k) * sin) * (d ** -0.5)
    log_g = jnp.log(1.0 - 2.0 ** (-5.0 - jnp.arange(H, dtype=jnp.float32)))

    def chunks(t):
        return t.reshape(B, N, C, H, t.shape[-1]).transpose(0, 3, 1, 2, 4)

    qc, kc, vc = chunks(q), chunks(k), chunks(v)
    idx = jnp.arange(C, dtype=jnp.float32)
    rel = idx[:, None] - idx[None, :]
    inner_decay = jnp.where(rel[None] >= 0,
                            jnp.exp(log_g[:, None, None] * jnp.maximum(rel, 0.0)[None]),
                            0.0)
    scores = jnp.einsum('bhncd,bhnmd->bhncm', qc, kc) * inner_decay[None, :, None]
    inner = jnp.einsum('bhncm,bhnme->bhnce', scores, vc)
    k_to_end = jnp.exp(log_g[:, None] * (C - 1 - idx)[None])
    chunk_state = jnp.einsum('bhnmd,bhnme->bhnde',
                             kc * k_to_end[None, :, None, :, None], vc)
    chunk_decay = jnp.exp(log_g * C)[None, :, None, None]

    def step(R, U):
        return R * chunk_decay + U, R

    _, R_prev = lax.scan(step, jnp.zeros((B, H, d, vc.shape[-1]), jnp.float32),
                         chunk_state.transpose(2, 0, 1, 3, 4))
    R_prev = R_prev.transpose(1, 2, 0, 3, 4)
    q_from_start = jnp.exp(log_g[:, None] * (idx + 1.0)[None])
    cross = jnp.einsum('bhncd,bhnde->bhnce', qc, R_prev) * q_from_start[None, :, None, :, None]
    return (inner + cross).transpose(0, 2, 3, 1, 4).reshape(B, S, H, vc.shape[-1])

def rwkv7_mix(h, mu, w0, w2, a0, a2, g2, k_k, k_a, r_k, ln_w, ln_b):
    B, S, _ = h.shape
    H, N, W = RWKV_HEADS, RWKV_HEAD_DIM, RWKV_WIDTH
    prev = jnp.pad(h, ((0, 0), (1, 0), (0, 0)))[:, :S]
    h = h + (prev - h) * mu
    r = h[..., :W]
    k = h[..., W:2 * W]
    v = h[..., 2 * W:3 * W]
    o = 3 * W
    wd = h[..., o:o + DECAY_LORA]
    o += DECAY_LORA
    ad = h[..., o:o + AAA_LORA]
    o += AAA_LORA
    gd = h[..., o:o + GATE_LORA]
    w_log = -jax.nn.softplus(-(w0 + jnp.tanh(wd) @ w2)) - 0.5
    decay = jnp.exp(-jnp.exp(w_log))
    a = jax.nn.sigmoid(a0 + ad @ a2)
    g = jax.nn.sigmoid(gd) @ g2

    def heads(t):
        return t.reshape(B, S, H, N)

    r, k, v, decay, a = heads(r), heads(k), heads(v), heads(decay), heads(a)
    kk = k * k_k.reshape(H, N)
    kk = kk * lax.rsqrt(jnp.maximum(jnp.sum(kk * kk, axis=-1, keepdims=True), 1e-24))
    k = k * (1.0 + (a - 1.0) * k_a.reshape(H, N))

    def step(state, inp):
        r_t, w_t, k_t, v_t, kk_t, b_t = inp
        sa = jnp.einsum('bhvk,bhk->bhv', state, -kk_t)
        state = (state * w_t[:, :, None, :] + sa[..., None] * b_t[:, :, None, :]
                 + v_t[..., None] * k_t[:, :, None, :])
        return state, jnp.einsum('bhvk,bhk->bhv', state, r_t)

    def tm(t):
        return jnp.swapaxes(t, 0, 1)

    _, y = lax.scan(step, jnp.zeros((B, H, N, N), jnp.float32),
                    (tm(r), tm(decay), tm(k), tm(v), tm(kk), tm(kk * a)))
    y = tm(y)
    y = head_norm(y, RWKV_GN_EPS).reshape(B, S, W) * ln_w + ln_b
    bonus = jnp.sum(r * k * r_k, axis=-1, keepdims=True) * v
    return (y + bonus.reshape(B, S, W)) * g

def second_inputs(seed: int = 0) -> dict:
    key = jax.random.key(seed)
    ks = jax.random.split(key, 32)
    f32 = jnp.float32

    def nrm(k, shape, scale):
        return jax.random.normal(k, shape, f32) * scale

    def gain(k, shape):
        return 1.0 + 0.02 * jax.random.normal(k, shape, f32)

    L = DEPTH
    return {
        "x": nrm(ks[0], (BATCH, SEQ, D_MODEL), 1.0),
        "p": nrm(ks[1], (DEPTH, BATCH, SEQ, D_PLE), 1.0),
        "norm_mix_w": gain(ks[2], (L, D_MODEL)),
        "w_in": nrm(ks[3], (L, D_MODEL, IN_COLS_2), D_MODEL ** -0.5),
        "ret_norm_w": gain(ks[4], (L, RET_WIDTH)),
        "rw_mu": jax.random.uniform(ks[5], (L, RWKV_COLS), f32, 0.0, 1.0),
        "rw_w0": jax.random.uniform(ks[6], (L, RWKV_WIDTH), f32, -6.0, 0.0),
        "rw_w2": nrm(ks[7], (L, DECAY_LORA, RWKV_WIDTH), 0.1 * DECAY_LORA ** -0.5),
        "rw_a0": nrm(ks[8], (L, RWKV_WIDTH), 0.1),
        "rw_a2": nrm(ks[9], (L, AAA_LORA, RWKV_WIDTH), 0.1 * AAA_LORA ** -0.5),
        "rw_g2": nrm(ks[10], (L, GATE_LORA, RWKV_WIDTH), GATE_LORA ** -0.5),
        "rw_k_k": 0.85 + 0.02 * jax.random.normal(ks[11], (L, RWKV_WIDTH), f32),
        "rw_k_a": gain(ks[12], (L, RWKV_WIDTH)),
        "rw_r_k": nrm(ks[13], (L, RWKV_HEADS, RWKV_HEAD_DIM), 0.1),
        "rw_ln_w": gain(ks[14], (L, RWKV_WIDTH)),
        "rw_ln_b": nrm(ks[15], (L, RWKV_WIDTH), 0.01),
        "w_o": nrm(ks[16], (L, D_MODEL, D_MODEL), D_MODEL ** -0.5),
        "norm_ffn_w": gain(ks[17], (L, D_MODEL)),
        "w_gate": nrm(ks[18], (L, D_MODEL, D_FF_2), D_MODEL ** -0.5),
        "w_up": nrm(ks[19], (L, D_MODEL, D_FF_2), D_MODEL ** -0.5),
        "w_down": nrm(ks[20], (L, D_FF_2, D_MODEL), D_FF_2 ** -0.5),
        "norm_ple_w": gain(ks[21], (L, D_MODEL)),
        "w_ple_gate": nrm(ks[22], (L, D_MODEL, D_MODEL), D_MODEL ** -0.5),
        "w_ple_up": nrm(ks[23], (L, D_PLE, D_MODEL), D_PLE ** -0.5),
        "final_norm_w": gain(ks[24], (D_MODEL,)),
    }

def second_block(x, p, norm_mix_w, w_in, ret_norm_w, rw_mu, rw_w0, rw_w2, rw_a0, rw_a2,
              rw_g2, rw_k_k, rw_k_a, rw_r_k, rw_ln_w, rw_ln_b, w_o, norm_ffn_w,
              w_gate, w_up, w_down, norm_ple_w, w_ple_gate, w_ple_up, final_norm_w):
    B, S, _ = x.shape
    for i in range(DEPTH):
        hn = rms_norm_2(x, norm_mix_w[i])
        proj = (hn @ w_in[i]).astype(jnp.float32)
        q = proj[..., 0:RET_WIDTH].reshape(B, S, RET_HEADS, RET_HEAD_DIM)
        k = proj[..., RET_WIDTH:2 * RET_WIDTH].reshape(B, S, RET_HEADS, RET_HEAD_DIM)
        v = proj[..., 2 * RET_WIDTH:3 * RET_WIDTH].reshape(B, S, RET_HEADS, RET_HEAD_DIM)
        ret_gate = proj[..., 3 * RET_WIDTH:RET_COLS]
        y_ret = head_norm(retention(q, k, v), RET_GN_EPS).reshape(B, S, RET_WIDTH)
        y_ret = y_ret * ret_norm_w[i] * jax.nn.silu(ret_gate)
        y_rw = rwkv7_mix(proj[..., RET_COLS:], rw_mu[i], rw_w0[i], rw_w2[i], rw_a0[i],
                         rw_a2[i], rw_g2[i], rw_k_k[i], rw_k_a[i], rw_r_k[i],
                         rw_ln_w[i], rw_ln_b[i])
        mixed = jnp.concatenate([y_ret, y_rw], axis=-1).astype(x.dtype)
        x = x + mixed @ w_o[i]
        hf = rms_norm_2(x, norm_ffn_w[i])
        x = x + (jax.nn.silu(hf @ w_gate[i]) * (hf @ w_up[i])) @ w_down[i]
        hp = rms_norm_2(x, norm_ple_w[i])
        x = x + (p[i] @ w_ple_up[i]) * jax.nn.sigmoid(hp @ w_ple_gate[i])
    return rms_norm_2(x, final_norm_w)


_first_inputs_2 = second_inputs


def second_inputs(seed=0):
    import zlib

    import numpy as np

    out = dict(_first_inputs_2(seed))
    spreads = {}
    factors = {'ret_norm_w': 7.627,
     'rw_w2': 8.0,
     'rw_a0': 4.119,
     'rw_a2': 4.142,
     'rw_k_k': 8.0,
     'rw_k_a': 8.0,
     'rw_ln_w': 8.0,
     'rw_ln_b': 8.0,
     'norm_ffn_w': 4.627,
     'norm_ple_w': 8.0,
     'final_norm_w': 2.85}
    for name, (base, spread) in spreads.items():
        noise = np.random.default_rng([zlib.crc32(name.encode()), seed]).standard_normal(out[name].shape)
        drawn = base * np.exp(spread * noise) if base else spread * noise
        out[name] = __import__('jax').numpy.asarray(drawn.astype(out[name].dtype))
    for name, factor in factors.items():
        out[name] = (out[name] * factor).astype(out[name].dtype)
    return out


_narrow_inputs_2 = second_inputs


def second_inputs(seed=0):

    out = dict(_narrow_inputs_2(seed))
    wider = {'ret_norm_w': 3.27,
     'rw_k_k': 3.65,
     'rw_ln_w': 3.39,
     'rw_ln_b': 6.77,
     'norm_ple_w': 12.0,
     'final_norm_w': 3.21}
    for name, times in wider.items():
        mean = out[name].mean()
        out[name] = (mean + times * (out[name] - mean)).astype(out[name].dtype)
    return out


def setup_inputs(seed=0):
    out = dict(first_inputs(seed))
    for name, value in second_inputs(seed + 1).items():
        if name != "x":
            out[name + "_2"] = value
    return out


def reference(
    x, meta, pre_mix_g, w_in, lambda_q1, lambda_k1, lambda_q2, lambda_k2, subln_g, a_re, a_im,
    log_dt, b_re, b_im, c_re, c_im, d_skip, w_glu, b_glu, ssm_out_g, w_out, post_mix_g,
    pre_ffn_g, w_gate, w_up, w_down, post_ffn_g, p_2, norm_mix_w_2, w_in_2, ret_norm_w_2,
    rw_mu_2, rw_w0_2, rw_w2_2, rw_a0_2, rw_a2_2, rw_g2_2, rw_k_k_2, rw_k_a_2, rw_r_k_2,
    rw_ln_w_2, rw_ln_b_2, w_o_2, norm_ffn_w_2, w_gate_2, w_up_2, w_down_2, norm_ple_w_2,
    w_ple_gate_2, w_ple_up_2, final_norm_w_2,
):
    x = first_block(
        x, meta, pre_mix_g, w_in, lambda_q1, lambda_k1, lambda_q2, lambda_k2, subln_g, a_re,
        a_im, log_dt, b_re, b_im, c_re, c_im, d_skip, w_glu, b_glu, ssm_out_g, w_out,
        post_mix_g, pre_ffn_g, w_gate, w_up, w_down, post_ffn_g,
    )
    return second_block(
        x, p_2, norm_mix_w_2, w_in_2, ret_norm_w_2, rw_mu_2, rw_w0_2, rw_w2_2, rw_a0_2, rw_a2_2,
        rw_g2_2, rw_k_k_2, rw_k_a_2, rw_r_k_2, rw_ln_w_2, rw_ln_b_2, w_o_2, norm_ffn_w_2,
        w_gate_2, w_up_2, w_down_2, norm_ple_w_2, w_ple_gate_2, w_ple_up_2, final_norm_w_2,
    )


_drawn_inputs = setup_inputs


def setup_inputs(seed=0):
    import zlib

    import numpy as np

    out = dict(_drawn_inputs(seed))
    spreads = {}
    factors = {}
    for name, (base, spread) in spreads.items():
        noise = np.random.default_rng([zlib.crc32(name.encode()), seed]).standard_normal(out[name].shape)
        drawn = base * np.exp(spread * noise) if base else spread * noise
        out[name] = __import__('jax').numpy.asarray(drawn.astype(out[name].dtype))
    for name, factor in factors.items():
        out[name] = (out[name] * factor).astype(out[name].dtype)
    return out
```

```python
import math
from contextlib import ExitStack

import numpy as np
import concourse.bass as bass
from concourse import mybir

F32, F32R, BF16 = mybir.dt.float32, mybir.dt.float32r, mybir.dt.bfloat16
ACT = mybir.ActivationFunctionType
ALU = mybir.AluOpType
X_AXIS = mybir.AxisListType.X
MUL, ADD, SUB = ALU.mult, ALU.add, ALU.subtract

P = 128
D = 1024
T = 1024
META = 16
L = META + T
KT = D // P
NT = T // P
BANK = 512
FF = 2816
FT = FF // P
EPS = 1e-6
HEADS, QK, VD = 4, 64, 128
ROT, THETA = QK // 4, 500000.0
LAM_INIT = 0.8 - 0.6 * math.exp(-0.3 * 0)
GROUPS, SG, SN = 32, 16, 64
STEP = 16
NSTEP = L // STEP
OCT = 8
NOCT = L // OCT
PAIRS = GROUPS // 2
GB = 8
LAGS = STEP + 1
RH, RD = 4, 128
WH, WN = 8, 64
CH = 64
RW_TILES = 14

SLOTS = 6
RAWS = 3
U_SSM, U_V, U_QK, U_GLU, U_OUT = 0, 4, 8, 16, 18
U_FF1 = U_OUT + 8
U_RW = U_FF1 + 3 * FT
U_RET = U_RW + RW_TILES
U_WO = U_RET + 16
U_FF2 = U_WO + 8
U_PLE = U_FF2 + 3 * FT
UNITS = U_PLE + 10

BASE = 16512
TOP = 229344
AT_ACT = BASE
AT_W = AT_ACT + 2 * KT * L * 4
AT_RAW = AT_W + 2 * SLOTS * 4096
AT_CONST = AT_RAW + RAWS * 4096
ARENA = AT_CONST + 7168

CLOSED = [0] + [NT + 1 + NT * c for c in range(6)]
H_MIX1, H_RET, H_WO, H_PLE, H_END = 0, 2, 6, 8, 12


class Tally:

    def __init__(self, eng):
        self.eng, self.given, self.taken = eng, {}, {}

    def post(self, ins, sem):
        ins.then_inc(sem, 1)
        self.given[sem.name] = self.given.get(sem.name, 0) + 1
        return self.given[sem.name]

    def give(self, ins, sem):
        self.eng.wait_ge(sem, self.post(ins, sem))

    def take(self, sem, k=1):
        n = self.taken[sem.name] = self.taken.get(sem.name, 0) + k
        self.eng.wait_ge(sem, n)


def build(nc, t):
    place = lambda name, shape, dt, at: nc.alloc_sbuf_tensor_at(name, shape, dt, offset=at)
    ctx = ExitStack()
    sem = lambda name: ctx.enter_context(nc.semaphore(name))

    act_hi = place("act_hi", [P, KT, L], F32R, AT_ACT)
    act_lo = place("act_lo", [P, KT, L], F32R, AT_ACT + KT * L * 4)
    w_hi = place("w_hi", [P, SLOTS, 1024], F32R, AT_W)
    w_lo = place("w_lo", [P, SLOTS, 1024], F32R, AT_W + SLOTS * 4096)
    w_raw = place("w_raw", [P, RAWS, 1024], F32, AT_RAW)
    ident = place("ident", [P, P], F32, AT_CONST)
    ones = place("ones", [P, P], F32, AT_CONST + 512)
    rot = place("rot", [P, P], F32, AT_CONST + 1024)
    causal = place("causal", [P, 2, P], BF16, AT_CONST + 1536)
    small = place("small", [P, 256], F32, AT_CONST + 2048)
    rope_sin_part = place("rope_sin_part", [P, BANK], F32, AT_CONST + 3072)
    lam_parts = place("lam_parts", [P, 4 * QK], F32, AT_CONST + 5120)
    eps_col = small[:, 255:256]
    ps = nc.alloc_psum_tensor("ps", [P, 8, BANK], F32)

    AT_CLOSE = TOP - 36864
    acc = place("acc", [P, NT, D], F32, ARENA)
    row = place("row", [P, 3, D], F32, AT_CLOSE)
    xn = place("xn", [P, 2, D], F32, AT_CLOSE + 12288)
    post_part = place("post_part", [P, D], F32, AT_CLOSE + 20480)
    squares = place("squares", [P, D], F32, AT_CLOSE + 24576)
    gain_next = place("gain_next", [P, D], F32, AT_CLOSE + 28672)
    gain_post = place("gain_post", [P, D], F32, AT_CLOSE + 32768)

    qk_t = place("qk_t", [P, 8, L], F32, ARENA)
    v_tok = place("v_tok", [P, NT + 1, HEADS * VD], F32, ARENA + 33280)
    u_t = place("u_t", [P, 2, OCT, NOCT], F32, ARENA + 51712)
    qk_raw = place("qk_raw", [P, 2, L], F32, ARENA + 60032)
    rope = place("rope", [P, 2, L], F32, ARENA + 68352)
    e_br = place("e_br", [P, 2, 2, L], F32, ARENA + 51712)
    a_t = place("a_t", [P, NT + 1, P], F32, ARENA + 68352)
    o_tile = place("o_tile", [P, 2, HEADS * VD], F32, ARENA + 72960)
    o_all = place("o_all", [P, NT, HEADS * VD], F32, ARENA)
    o_sq = place("o_sq", [P, HEADS * VD], F32, ARENA + 16384)
    o_n = place("o_n", [P, 2, HEADS * VD], F32, ARENA + 18432)
    sub_gain = place("sub_gain", [P, VD], F32, ARENA + 22528)

    w_landed = [sem(f"w_landed_{r}") for r in range(RAWS)]
    w_hi_made, w_ready, unit_done = sem("w_hi_made"), sem("w_ready"), sem("unit_done")
    act_step, dve_step = sem("act_step"), sem("dve_step")
    const_landed, gain_landed = sem("const_landed"), sem("gain_landed")
    row_landed = [sem(f"row_landed_{r}") for r in range(3)]
    row_stored = [sem(f"row_stored_{r}") for r in range(3)]
    post_root, row_root, row_final = sem("post_root"), sem("row_root"), sem("row_final")
    xn_ready, turned, hi_done, act_ready = sem("xn_ready"), sem("turned"), sem("hi_done"), sem("act_ready")
    u_evac = sem("u_evac")
    u_stored = [sem(f"u_stored_{r}") for r in range(2)]
    v_psum, v_ready = sem("v_psum"), sem("v_ready")
    qk_raw_ready, rot_psum, rope_done = sem("qk_raw_ready"), sem("rot_psum"), sem("rope_done")
    lam_sums, lam_exp, eps_ready, down_added = sem("lam_sums"), sem("lam_exp"), sem("eps_ready"), sem("down_added")
    s_psum, s_max, s_exp, a_ready = sem("s_psum"), sem("s_max"), sem("s_exp"), sem("a_ready")
    at_psum, at_ready, o_psum, o_ready = sem("at_psum"), sem("at_ready"), sem("o_psum"), sem("o_ready")
    o_stored = [sem(f"o_stored_{r}") for r in range(2)]
    o_landed = sem("o_landed")
    sub_root, sub_ms, sub_normed, sub_turned, sub_hi, sub_lo = (
        sem("sub_root"), sem("sub_ms"), sem("sub_normed"), sem("sub_turned"), sem("sub_hi"), sem("sub_lo"))
    rope_landed = sem("rope_landed")

    PASSES = ((0, 0), (0, 1), (1, 0))
    acts, ws = (act_hi, act_lo), (w_hi, w_lo)
    row_source = [t["x"], t["x"], t["res"], t["res"], t["res"], t["res"]]
    post_gain = [None, "post_mix_g", "post_ffn_g", None, None, None]
    GAINS = [1, 3, 5, 6, 7, 8]
    next_gain = ["pre_mix_g", "pre_ffn_g", "norm_mix_w_2", "norm_ffn_w_2", "norm_ple_w_2", "final_norm_w_2"]

    def tiles_of(c):
        if c == 0:
            return [(0, META, None, 0)] + [(1 + i, P, P * i, META + P * i) for i in range(NT)]
        return [(CLOSED[c] + i, P, P * i, META + P * i) for i in range(NT)]

    SPAN_BANKS = ((0, 1, 4), (2, 3, 5))
    SPANS = ((META, META + BANK), (META + BANK, L), (0, META))
    ROPE_GROUPS = [2 * (m + 1) + max(0, m - 3) for m in range(8)]
    WIDE = (NT - 1) * HEADS
    key_batches = lambda qi: [(k, min(4, qi + 1 - k)) for k in range(0, qi + 1, 4)] + [(NT, 1)]
    TURNS = [0]
    for unit in range(NT * HEADS):
        TURNS.append(TURNS[-1] + len(key_batches(unit // HEADS)))

    def score_rows(qi, br, n):
        first, banks = (3 * br, 3) if qi == NT - 1 else (2 * br, 2)
        return ps[:, first:first + banks, :].rearrange("p b n -> p (b n)")[:, 0:n]

    output_bank = lambda unit: 7 if unit >= WIDE else 6 + unit % 2
    turn_bank = lambda unit, n: 6 if unit >= WIDE else 4 + n % 2


    u_in = place("u_in", [P, GROUPS, NOCT], F32, ARENA)
    xs = place("xs", [P, 2, PAIRS, NSTEP + 1], F32, ARENA + 16640)
    ssm_vec = place("ssm_vec_s", [P, 3, PAIRS], F32, ARENA + 25088)
    wv = place("wv", [P, 24, PAIRS], F32, ARENA + 25280)
    b_t = place("b_t", [P, 2, PAIRS, SG], F32, ARENA + 26816)
    c_t = place("c_t", [P, 2, PAIRS, SG], F32, ARENA + 28864)
    bb = place("bb", [P, 2, PAIRS, SG], F32, ARENA + 30912)
    pw = place("pw", [P, 2, PAIRS, LAGS], F32, ARENA + 32960)
    a16 = place("a16", [P, 2, 2, PAIRS], F32, ARENA + 35136)
    d_t = place("d_t", [SG, GROUPS, SG], F32, ARENA + 35392)
    ca = place("ca", [P, 2, 4, LAGS, SG], F32, ARENA + 37440)
    cab = place("cab", [P, 2, 4 * LAGS * SG], F32, ARENA + 46144)
    g_t = place("g_t", [P, 2, 4, STEP, SG], F32, ARENA + 54848)
    gt = place("gt", [P, 4, 2, 2, P], F32, ARENA + 63040)
    kd = place("kd", [SG, 4, 24 * SG], F32, ARENA + 71232)
    ca2 = place("ca2", [P, 2, 2, 4, LAGS, SG], F32, ARENA + 37440)
    m_t = place("m_t", [P, 2, GB, 2 * P], F32, ARENA + 54848)
    yb = place("yb", [P, 2, GB, NOCT], F32, ARENA + 26816)
    y_raw = place("y_raw", [P, 4, OCT, P], F32, ARENA)
    yh = place("yh", [P, 4, T], F32R, ARENA + 16384)
    yl = place("yl", [P, 4, T], F32R, ARENA + 32768)
    sig = place("sig", [P, 2, T], F32, ARENA + 49152)
    ysq = place("ysq", [P, 2, T], F32, ARENA + 57344)
    rinv = place("rinv", [P, T], F32, ARENA + 65536)
    glu_vec = small[:, 192:200]
    ssm_landed, ssm_fn, ssm_arg = sem("ssm_landed"), sem("ssm_fn"), sem("ssm_arg")
    bb_ready = sem("bb_ready")
    ca_ready, ca_stored, g_ready, g_turned, gt_ready = sem("ca_ready"), sem("ca_stored"), sem("g_ready"), sem("g_turned"), sem("gt_ready")
    kd_psum, kd_ready, kd_stored, ssm_s, ssm_x, ssm_scanned = (
        sem("kd_psum"), sem("kd_ready"), sem("kd_stored"), sem("ssm_s"), sem("ssm_x"), sem("ssm_scanned"))
    tab_landed = [sem("tab_landed_0"), sem("tab_landed_1")]
    y_psum, y_gelu, y_landed = sem("y_psum"), sem("y_gelu"), sem("y_landed")
    y_stored = [sem("y_stored_0"), sem("y_stored_1")]
    y_hi, y_lo, glu_psum, glu_sig, glu_sq, glu_sum, glu_root, glu_prod, glu_hi, glu_lo = (
        sem("y_hi"), sem("y_lo"), sem("glu_psum"), sem("glu_sig"), sem("glu_sq"), sem("glu_sum"), sem("glu_root"),
        sem("glu_prod"), sem("glu_hi"), sem("glu_lo"))

    ffh = [place("ffh_hi", [P, 2, T], F32R, AT_CLOSE), place("ffh_lo", [P, 2, T], F32R, AT_CLOSE + 8192)]
    ff_f = place("ff_f", [P, 2, T], F32, AT_CLOSE + 16384)
    tok_psum, tok_done = sem("tok_psum"), sem("tok_done")
    ff_silu, ff_prod, ff_hi, ff_lo, down_psum = sem("ff_silu"), sem("ff_prod"), sem("ff_hi"), sem("ff_lo"), sem("down_psum")
    down_base = lambda f: 4 + f * (16 * FT + 4)

    rw_t = place("rw_t", [P, 2, T], F32, ARENA)
    rw_masks = place("rw_masks_s", [P, 7, P], F32, AT_CONST + 3072)
    head_ones = place("head_ones_s", [P, P], F32, AT_CONST + 1024)
    rw_vec = place("rw_vec_s", [P, 64], F32, AT_CONST + 6656)
    id2 = place("id2", [P, CH], F32, AT_CONST + 6912)
    rw_consts, rw_one, rw_mixed, rw_evac = sem("rw_consts"), sem("rw_one"), sem("rw_mixed"), sem("rw_evac")
    rw_stored = [sem("rw_stored_0"), sem("rw_stored_1")]
    rq = place("rq", [P, NT, RH * RD], F32, ARENA)
    rk = place("rk", [P, NT, RH * RD], F32, ARENA + 16384)
    rv = place("rv", [P, NT, RH * RD], F32, ARENA + 32768)
    ret_cos = place("ret_cos_s", [P, NT, RD // 2], F32, ARENA + 49152)
    ret_sin = place("ret_sin_s", [P, NT, RD // 2, 2], F32, ARENA + 51200)
    ret_decay = place("ret_decay_s", [P, RH, P], F32, ARENA + 55296)
    ret_start = place("ret_start_s", [P, RH, P], F32, ARENA + 57344)
    q_t = place("q_t", [P, RH, P], F32, ARENA + 59392)
    qs_t = place("qs_t", [P, RH, P], F32, ARENA + 61440)
    k_t = place("k_t", [P, RH, P], F32, ARENA + 63488)
    k_end = place("k_end", [P, RH, RD], F32, ARENA + 65536)
    s_t = place("s_t", [P, RH, P], F32, ARENA + 67584)
    r_state = place("r_state", [P, RH, RD], F32, ARENA + 69632)
    ry = place("ry", [P, RH, RD], F32, ARENA + 71680)
    rg_in = place("rg_in", [P, RH * RD], F32, ARENA + 73728)
    ret_norm = place("ret_norm_s", [P, RH * RD], F32, AT_CONST + 3072)
    ret_end = small[:, 200:204]
    eps5 = small[:, 253:254]
    eps64 = small[:, 254:255]
    rg_out = place("rg_out", [P, 2, RH * RD], F32, ARENA + 61440)
    ret_landed, rot_done, g_landed = sem("ret_landed"), sem("rot_done"), sem("g_landed")
    rg_stored = [sem("rg_stored_0"), sem("rg_stored_1")]
    c_turned, c_q, c_qs, c_k, c_kend, sc_psum, sc_ready, ret_psum, ret_u, ret_state = (
        sem("c_turned"), sem("c_q"), sem("c_qs"), sem("c_k"), sem("c_kend"), sem("sc_psum"), sem("sc_ready"), sem("ret_psum"),
        sem("ret_u"), sem("ret_state"))
    ret_var, ret_root, ret_y, ret_turned, ret_hi, ret_lo = (
        sem("ret_var"), sem("ret_root"), sem("ret_y"), sem("ret_turned"), sem("ret_hi"), sem("ret_lo"))
    GAMMA = [1.0 - 2.0 ** (-5.0 - h) for h in range(RH)]

    def tok_cols(i):
        return slice(META + P * i, META + P * i + P)


    rk_ = place("removal_reading", [P, 2, T], F32, ARENA)
    bh = place("added", [P, 2, T], F32, ARENA + 8192)
    to_end = place("to_end", [P, 2, T], F32, ARENA + 16384)
    vv = place("vv", [P, T], F32, ARENA + 24576)
    gg = place("gg", [P, T], F32, ARENA + 28672)
    bonus = place("bonus", [P, T], F32, ARENA + 32768)
    wa = place("wa", [P, T], F32, ARENA + 36864)
    sgd = place("sgd", [P, T], F32, ARENA + 40960)
    lc = place("lc", [P, T], F32, ARENA + 45056)
    aa = place("aa", [P, T], F32, ARENA + 49152)
    work = place("work", [P, T], F32, ARENA + 53248)
    cum = place("cum", [P, T], F32, ARENA + 57344)
    kraw = place("kraw", [P, T], F32, ARENA + 61440)
    lora = place("lora", [P, 2, P], F32, ARENA + 65536)
    run = place("run", [P, T], F32, ARENA + 69632)
    toks = place("toks", [P, 3, 2, P], F32, ARENA + 45056)
    n_m = place("n_m", [P, 4, 2, P], F32, ARENA + 49152)
    k_m = place("k_m", [P, 4, 2, P], F32, ARENA + 53248)
    n_t = place("n_t", [P, 4, P], F32, ARENA + 57344)
    inv = place("inv", [P, 4, P], F32, ARENA + 59392)
    xp = [place("xp_0", [P, 4, P], F32, ARENA + 61440), place("xp_1", [P, 4, P], F32, ARENA + 63488)]
    xt = [place("xt_0", [P, 4, P], F32, ARENA + 65536), place("xt_1", [P, 4, P], F32, ARENA + 67584)]
    km = place("km", [P, 4, P], F32, ARENA + 69632)
    wu = place("wu", [P, 4, P], F32, ARENA + 71680)
    rwt = place("rwt", [P, 2, P], F32, ARENA + 73728)
    ac = place("ac", [P, 2, 2, CH], F32, ARENA + 74752)
    bc = place("bc", [P, 2, 2, CH], F32, ARENA + 75776)
    y0 = place("y0", [P, 4, CH], F32, ARENA + 71680)
    yn = place("yn", [P, 2, 2, CH], F32, ARENA + 72704)
    yo = place("yo", [P, 2, P], F32, ARENA + 48128)
    state = place("state", [P, 2, CH], F32, AT_CONST + 1536)
    chunk_decay = small[:, 213:229]
    v4, m4 = small[:, 229:233], small[:, 233:237]
    C_DECAY = math.exp(-0.5)
    GG = NT // 2
    wk_names = ("landed", "lora", "pre", "fn", "arg", "sums", "sq2", "lora_in", "mats", "toks", "kept_act", "kept_dve", "square", "z",
                "merge", "wu", "parts", "step", "state", "var", "root", "yt", "out", "hi", "lo")
    (wk_landed, wk_lora, wk_pre, wk_fn, wk_arg, wk_sums, wk_sq2, wk_lora_in, wk_mats, wk_toks, wk_kept_act, wk_kept_dve, wk_square, wk_z,
     wk_merge, wk_wu, wk_parts, wk_step, wk_state, wk_var, wk_root, wk_yt, wk_out, wk_hi, wk_lo) = [sem("wk_" + n) for n in wk_names]

    p_raw = place("p_raw", [P, 2, T], F32, AT_CLOSE)
    p_parts = [place("p_hi", [P, 2, T], F32R, AT_CLOSE + 8192), place("p_lo", [P, 2, T], F32R, AT_CLOSE + 16384)]
    p_landed, p_hi_made, p_ready, ple_done = sem("p_landed"), sem("p_hi_made"), sem("p_ready"), sem("ple_done")
    out_stored = [sem("out_stored_0"), sem("out_stored_1")]

    def both(bank):
        return ps[:, bank:bank + 2, :].rearrange("p b n -> p (b n)")

    def four(bank, n=P):
        return ps[:, bank, 0:4 * n].rearrange("p (u n) -> p u n", u=4)

    block = ctx.enter_context(nc.Block())

    @block.sync
    def _(sp):
        def load(i, s):
            u = i * SLOTS + s
            if not isinstance(i, int) or u >= RAWS:
                sp.wait_ge(w_ready, u - RAWS + 1)
            sp.dma_start(w_raw[:, s % RAWS], t["weights"][u]).then_inc(w_landed[s % RAWS], 16)

        for s in range(SLOTS):
            load(0, s)
        with sp.Fori(1, UNITS // SLOTS) as i:
            for s in range(SLOTS):
                load(i, s)
        for s in range(UNITS % SLOTS):
            load(UNITS // SLOTS, s)

    @block.gpsimd
    def _(pool):
        def split(i, s):
            u = i * SLOTS + s
            pool.wait_ge(w_landed[s % RAWS], 16 * (i * (SLOTS // RAWS) + s // RAWS + 1))
            if not isinstance(i, int) or u >= SLOTS:
                pool.wait_ge(unit_done, u - SLOTS + 1)
            pool.tensor_tensor(w_hi[:, s], w_raw[:, s % RAWS], ones[:, 0:1].to_broadcast([P, 1024]), MUL).then_inc(w_hi_made, 1)
            pool.wait_ge(w_hi_made, u + 1)
            pool.tensor_tensor(w_lo[:, s], w_raw[:, s % RAWS], w_hi[:, s].bitcast(F32), SUB).then_inc(w_ready, 1)

        pool.wait_ge(const_landed, 16 * 5)
        for s in range(SLOTS):
            split(0, s)
        with pool.Fori(1, UNITS // SLOTS) as i:
            for s in range(SLOTS):
                split(i, s)
        for s in range(UNITS % SLOTS):
            split(UNITS // SLOTS, s)

    @block.scalar
    def _(act):
        tally = Tally(act)
        give, post, take = tally.give, tally.post, tally.take
        loads = [0, 0, 0]
        stores = [0, 0, 0]

        def fn(out, in_, func, **kw):
            return act.activation(out, in_, func, **kw)

        def load_consts():
            for dst, name in ((ident[:, :], "ident"), (ones[:, :], "ones"), (rot[:, :], "rot"), (causal[:, :, :], "causal"),
                              (lam_parts[:, :], "lam_vectors")):
                act.dma_start(dst, t[name]).then_inc(const_landed, 16)

        def load_row(c, n):
            g, rows, r0, _ = tiles_of(c)[n]
            src = t["meta"] if r0 is None else row_source[c][r0:r0 + P, :]
            slot = g % 3
            if stores[slot]:
                act.wait_ge(row_stored[slot], 16 * stores[slot])
            act.dma_start(row[0:rows, slot], src).then_inc(row_landed[slot], 16)
            loads[slot] += 1

        def residual(c):
            tiles = tiles_of(c)
            if c:
                act.wait_ge(xn_ready, CLOSED[c])
                act.wait_ge(act_ready, CLOSED[c])
            if c in (2, 4):
                act.wait_ge(down_added, down_base(c // 2 - 1) + 16 * FT)
            if post_gain[c]:
                act.dma_start(gain_post[:, :], t[post_gain[c]].partition_broadcast(P)).then_inc(gain_landed, 16)
            act.dma_start(gain_next[:, :], t[next_gain[c]].partition_broadcast(P)).then_inc(gain_landed, 16)
            for n in range(3):
                load_row(c, n)
            for step in range(len(tiles) + 2):
                if step < len(tiles) and post_gain[c]:
                    g, rows, _, _ = tiles[step]
                    give(fn(squares[:, :], acc[:, step], ACT.Square, accum_out=small[:, g % 64:g % 64 + 1]), act_step)
                    post(fn(small[:, g % 64:g % 64 + 1], small[:, g % 64:g % 64 + 1], ACT.Sqrt, bias=eps_col, scale=1.0 / D), post_root)
                if 1 <= step <= len(tiles):
                    g, rows, r0, _ = tiles[step - 1]
                    if c:
                        act.wait_ge(row_final, g - NT)
                        if c < 5:
                            act.dma_start(t["res"][r0:r0 + P, :], row[:, g % 3]).then_inc(row_stored[g % 3], 16)
                            stores[g % 3] += 1
                    else:
                        act.wait_ge(row_landed[g % 3], 16 * (g // 3 + 1))
                    if c == 0 and step == 1:
                        act.wait_ge(eps_ready, 1)
                    ss = small[0:rows, 64 + g % 64:65 + g % 64]
                    give(fn(squares[0:rows, :], row[0:rows, g % 3], ACT.Square, accum_out=ss), act_step)
                    give(fn(ss, ss, ACT.Sqrt, bias=eps_col[0:rows], scale=1.0 / D), row_root)
                if step >= 2 and c < 5:
                    g, rows, _, c0 = tiles[step - 2]
                    act.wait_ge(turned, g + 1)
                    if rows == META:
                        give(fn(act_hi[:, :, 0:META], ps[:, 0, 0:KT * META].rearrange("p (k n) -> p k n", k=KT), ACT.Copy), hi_done)
                    else:
                        for b in range(2):
                            bank = 2 * (g % 2) + b
                            fin = fn(act_hi[:, 4 * b:4 * b + 4, c0:c0 + P], ps[:, bank, :].rearrange("p (k n) -> p k n", k=4), ACT.Copy)
                            post(fin, act_step) if b == 0 else give(fin, hi_done)
                if step >= 2 and c == 5:
                    g, _, r0, _ = tiles[step - 2]
                    act.wait_ge(xn_ready, g + 1)
                    act.dma_start(t["out"][r0:r0 + P, :], xn[:, g % 2]).then_inc(out_stored[g % 2], 16)
                if step >= 2 and step + 1 < len(tiles):
                    act.wait_ge(xn_ready, tiles[step - 2][0] + 1)
                    load_row(c, step + 1)
            for s in range(3):
                if stores[s]:
                    act.wait_ge(row_stored[s], 16 * stores[s])
            if c == 5:
                for s in range(2):
                    act.wait_ge(out_stored[s], 16 * NT // 2)

        def first_projection():
            act.wait_ge(act_ready, CLOSED[1])
            act.dma_start(rope[:, :, :], t["rope"]).then_inc(rope_landed, 16)
            for m in range(4):
                if m >= 2:
                    act.wait_ge(u_stored[m % 2], 16 * (m // 2))
                act.wait_ge(unit_done, U_SSM + m + 1)
                for h in range(3):
                    n = META if h == 2 else BANK
                    o0 = 0 if h == 2 else (META + BANK * h) // OCT
                    give(fn(u_t[:, m % 2, :, o0:o0 + n // OCT].rearrange("p s c -> p c s"),
                            ps[:, SPAN_BANKS[m % 2][h], 0:n].rearrange("p (c s) -> p c s", s=OCT), ACT.Copy), u_evac)
                act.dma_start(t["u_scratch"][m], u_t[:, m % 2]).then_inc(u_stored[m % 2], 16)
            for i in range(NT + 1):
                if i < NT:
                    take(v_psum)
                else:
                    act.wait_ge(unit_done, U_V + 4)
                rows = META if i == NT else P
                give(fn(v_tok[0:rows, i], ps[0:rows, 6 + i % 2, :], ACT.Copy), v_ready)
            for m in range(8):
                if m >= 2:
                    act.wait_ge(rope_done, ROPE_GROUPS[m - 2])
                if m == 0:
                    for r in range(2):
                        act.wait_ge(u_stored[r], 32)
                act.wait_ge(unit_done, U_QK + m + 1)
                for h in range(2 + (m >= 4)):
                    n = META if h == 2 else BANK
                    c0 = 0 if h == 2 else META + BANK * h
                    give(fn(qk_raw[:, m % 2, c0:c0 + n], ps[:, SPAN_BANKS[m % 2][h], 0:n], ACT.Copy,
                            scale=QK ** -0.5 if m < 4 else 1.0), qk_raw_ready)

        def attention():
            take(lam_sums)
            give(fn(small[:, 130:132], small[:, 128:130], ACT.Exp), lam_exp)
            act.wait_ge(rope_done, ROPE_GROUPS[7])
            for unit in range(NT * HEADS):
                qi, h = unit // HEADS, unit % HEADS
                n = (qi + 1) * P + META
                if unit >= 2:
                    act.wait_ge(at_psum, TURNS[unit - 1])
                for br in range(2):
                    take(s_max)
                    col = 140 + 4 * (unit % 2) + br
                    give(fn(e_br[:, unit % 2, br, 0:n], score_rows(qi, br, n), ACT.Exp,
                            bias=small[:, col:col + 1], accum_out=small[:, col + 2:col + 3]), s_exp)
                if unit:
                    output(unit - 1)
            output(NT * HEADS - 1)

        def output(unit):
            qi, h = unit // HEADS, unit % HEADS
            take(o_psum)
            if h == 0 and qi >= 2:
                act.wait_ge(o_stored[qi % 2], 16 * (qi // 2))
            give(fn(o_tile[:, qi % 2, h * VD:(h + 1) * VD], ps[:, output_bank(unit), 0:VD], ACT.Copy), o_ready)
            if h == HEADS - 1:
                act.dma_start(t["o_scratch"][qi], o_tile[:, qi % 2]).then_inc(o_stored[qi % 2], 16)

        def attention_norm():
            for r in range(2):
                act.wait_ge(o_stored[r], 16 * (NT // 2))
            act.dma_start(o_all[:, :, :], t["o_scratch"].rearrange("i p n -> p i n")).then_inc(o_landed, 16)
            act.dma_start(sub_gain[:, :], t["subln_g"].partition_broadcast(P)).then_inc(o_landed, 16)
            take(sub_ms)
            give(fn(small[:, 160:192], small[:, 160:192], ACT.Sqrt, bias=eps_col, scale=1.0 / VD), sub_root)
            for i in range(NT):
                take(sub_turned)
                give(fn(act_hi[:, 0:4, META + P * i:META + P * i + P],
                        ps[:, i % 2, :].rearrange("p (k n) -> p k n", k=4), ACT.Copy), sub_hi)

        def ssm_tables():
            for s in range(OCT):
                act.dma_start(u_in[SG * s:SG * s + SG], t["u_scratch"][:, :, s, :].rearrange("m (g h) c -> h (m g) c", h=SG)).then_inc(ssm_landed, 16)
            for dst, name in ((ssm_vec[:, :, :], "ssm_vec"), (b_t[:, :, :, :], "ssm_b"), (c_t[:, :, :, :], "ssm_c"),
                              (d_t[:, :, :], "ssm_d"), (glu_vec, "glu_vec")):
                act.dma_start(dst, t[name]).then_inc(ssm_landed, 16)
            act.wait_ge(ssm_landed, 16 * 13)
            give(fn(wv[:, 0], ssm_vec[:, 2], ACT.Exp), ssm_fn)
            take(ssm_arg)
            give(fn(wv[:, 1], wv[:, 1], ACT.Exp), ssm_fn)
            give(fn(wv[:, 3:5], wv[:, 3:5], ACT.Sin), ssm_fn)
            for b in range(4):
                act.wait_ge(ca_ready, b + 1)
                act.dma_start(t["ca_scratch"][b], ca[:, :, :, :, :]).then_inc(ca_stored, 16)
                for n in range(2):
                    act.wait_ge(kd_ready, 2 * b + n + 1)
                    act.dma_start(t["kd_scratch"][:, GB * b + 4 * n:GB * b + 4 * n + 4, :], kd[:, :, :]).then_inc(kd_stored, 16)

        def load_tables(b):
            act.dma_start(ca2[:, b % 2], t["ca_scratch"][b]).then_inc(tab_landed[b % 2], 16)
            for s in range(OCT):
                act.dma_start(m_t[SG * s:SG * s + SG, b % 2], t["kd_scratch"][:, GB * b:GB * b + GB, SG * (OCT - s):SG * (OCT - s) + 2 * P])\
                   .then_inc(tab_landed[b % 2], 16)

        def ssm_outputs():
            act.wait_ge(ca_stored, 16 * 4)
            act.wait_ge(kd_stored, 16 * 8)
            act.wait_ge(ssm_x, 4)
            load_tables(0)
            load_tables(1)
            for b in range(4):
                if b >= 2:
                    act.wait_ge(y_stored[b % 2], 16)
                if b == 0:
                    act.wait_ge(ssm_scanned, 1)
                for j in range(GB):
                    take(y_psum)
                    give(fn(yb[:, b % 2, j].rearrange("p (c k) -> p k c", k=2), ps[:, j, 0:NOCT].rearrange("p (k c) -> p k c", k=2), ACT.Gelu), y_gelu)
                act.dma_start(t["y_scratch"][:, GB * b:GB * b + GB, :], yb[:, b % 2]).then_inc(y_stored[b % 2], 16)
                if b < 2:
                    load_tables(b + 2)
            for r in range(2):
                act.wait_ge(y_stored[r], 32)
            y_view = t["y_scratch"].rearrange("(t h) g c -> h t g c", h=SG)
            for m in range(4):
                for j in range(GB):
                    act.dma_start(y_raw[SG * j:SG * j + SG, m], y_view[:, :, GB * m + j, META // OCT:NOCT]).then_inc(y_landed, 16)

        def glu():
            act.wait_ge(y_landed, 16 * 32)
            for m in range(4):
                give(fn(yh[:, m], y_raw[:, m].rearrange("p t c -> p (t c)"), ACT.Copy), y_hi)
            for m in range(4):
                if m % 2:
                    act.wait_ge(unit_done, U_GLU + m // 2 + 1)
                else:
                    take(glu_psum)
                if m >= 2:
                    act.wait_ge(glu_prod, m - 1)
                give(fn(sig[:, m % 2], ps[:, 2 * (m % 2):2 * (m % 2) + 2, :].rearrange("p b n -> p (b n)"), ACT.Sigmoid,
                        bias=glu_vec[:, m:m + 1]), glu_sig)
            act.wait_ge(glu_sum, 4)
            give(fn(rinv[:, :], ps[:, 4:6, :].rearrange("p b n -> p (b n)"), ACT.Sqrt, bias=eps_col, scale=1.0 / (4 * P)), glu_root)
            for m in range(4):
                act.wait_ge(glu_prod, 4 + m + 1)
                give(fn(act_hi[:, 4 + m, META:L].rearrange("p (c t) -> p t c", t=OCT), y_raw[:, m], ACT.Copy), glu_hi)

        def token_sums(half, unit, out, func=ACT.Copy, signal=None, scale=1.0):
            for i in range(NT):
                if i < NT - 1:
                    act.wait_ge(tok_psum, (NT - 1) * half + i + 1)
                else:
                    act.wait_ge(unit_done, unit + 1)
                give(fn(out(i), ps[:, i, :], func, scale=scale), tok_done)

        def feed_forward(f, u0):
            def tile(n, slot, gate_unit):
                act.wait_ge(unit_done, gate_unit + 1)
                if not isinstance(n, int) or n >= 1:
                    act.wait_ge(ff_lo, n + FT * f)
                act.activation(ff_f[:, slot], ps[:, 0:2, :].rearrange("p b n -> p (b n)"), ACT.Silu).then_inc(ff_silu, 1)
                act.wait_ge(ff_prod, n + (FT * f + 1))
                act.activation(ffh[0][:, slot], ff_f[:, slot], ACT.Copy).then_inc(ff_hi, 1)

            tile(0, 0, u0)
            with act.Fori(0, (FT - 2) // 2) as i:
                for s in range(2):
                    tile(i * 2 + (1 + s), (1 + s) % 2, i * 6 + (u0 + 2 + 3 * s))
            tile(FT - 1, 1, u0 + 2 + 3 * (FT - 2))

        def rw_projection():
            act.wait_ge(row_final, CLOSED[3] - (NT + 1))
            for dst, name in ((head_ones[:, :], "head_ones"), (rw_vec[:, 0:42], "rw_vec")):
                act.dma_start(dst, t[name]).then_inc(rw_consts, 16)
            act.wait_ge(rw_one, 1)
            for m in range(RW_TILES):
                if m >= 2:
                    act.wait_ge(rw_stored[m % 2], 16 * (m // 2))
                act.wait_ge(unit_done, U_RW + m + 1)
                give(fn(rw_t[:, m % 2], ps[:, 2 * (m % 2):2 * (m % 2) + 2, :].rearrange("p b n -> p (b n)"), ACT.Copy,
                        scale=rw_vec[:, 42 + m:43 + m]), rw_evac)
                act.wait_ge(rw_mixed, m + 1)
                act.dma_start(t["rw"][m], rw_t[:, m % 2]).then_inc(rw_stored[m % 2], 16)

        def retention():
            for r in range(2):
                act.wait_ge(rw_stored[r], 16 * (RW_TILES // 2))
            for dst, name in ((ret_cos[:, :, :], "ret_cos"), (ret_sin[:, :, :, :], "ret_sin"), (ret_decay[:, :, :], "ret_decay"),
                              (ret_start[:, :, :], "ret_start"), (ret_end, "ret_end")):
                act.dma_start(dst, t[name]).then_inc(ret_landed, 16)
            act.dma_start(ret_norm[:, :], t["ret_norm"].partition_broadcast(P)).then_inc(ret_landed, 16)
            token_sums(H_RET, U_RET + 3, lambda i: rq[:, i])
            token_sums(H_RET + 1, U_RET + 7, lambda i: rk[:, i], scale=RD ** -0.5)
            token_sums(H_RET + 2, U_RET + 11, lambda i: rv[:, i])
            for i in range(NT):
                half = H_RET + 3
                if i < NT - 1:
                    act.wait_ge(tok_psum, (NT - 1) * half + i + 1)
                else:
                    act.wait_ge(unit_done, U_RET + 16)
                if i >= 2:
                    act.wait_ge(rg_stored[i % 2], 16 * (i // 2))
                give(fn(rg_out[:, i % 2], ps[:, i, :], ACT.Silu), tok_done)
                act.dma_start(t["g_scratch"][i], rg_out[:, i % 2]).then_inc(rg_stored[i % 2], 16)
            for r in range(2):
                act.wait_ge(rg_stored[r], 16 * (NT // 2))
            def front(i):
                act.wait_ge(c_turned, 2 * i + 1)
                give(fn(q_t[:, :, :], ps[:, 0, :].rearrange("p (h n) -> p h n", h=RH), ACT.Copy), c_q)
                act.wait_ge(c_turned, 2 * i + 2)
                give(fn(k_t[:, :, :], ps[:, 1, :].rearrange("p (h n) -> p h n", h=RH), ACT.Copy), c_k)

            front(0)
            for i in range(NT):
                if i:
                    act.wait_ge(ret_y, i)
                act.dma_start(rg_in[:, :], t["g_scratch"][i]).then_inc(g_landed, 16)
                if i + 1 < NT:
                    front(i + 1)
                take(ret_var)
                give(fn(small[:, 204:208], small[:, 204:208], ACT.Sqrt, bias=eps5, scale=1.0 / RD), ret_root)
                take(ret_turned)
                give(fn(act_hi[:, 0:4, tok_cols(i)], ps[:, 5, :].rearrange("p (k n) -> p k n", k=4), ACT.Copy), ret_hi)

        def rwkv_pair(j):
            if j:
                act.wait_ge(wk_lo, GG * j)
            for dst, src in ((rk_[:, 1], t["rw"][j]), (kraw[:, :], t["rw"][4 + j]), (vv[:, :], t["rw"][8 + j]),
                             (lora[:, 0], t["rw_w2a2"][:, P * j:P * j + P]), (lora[:, 1], t["rw_g2"][:, P * j:P * j + P])):
                act.dma_start(dst, src).then_inc(wk_landed, 16)
            act.wait_ge(wk_lora, j + 1)
            give(fn(lc[:, :], both(0), ACT.Sigmoid, bias=rw_vec[:, 14 + j:15 + j]), wk_fn)
            give(fn(aa[:, :], both(2), ACT.Sigmoid, bias=rw_vec[:, 18 + j:19 + j]), wk_fn)
            give(fn(gg[:, :], both(4), ACT.Copy), wk_fn)
            take(wk_arg)
            give(fn(work[:, :], work[:, :], ACT.Exp, scale=-C_DECAY), wk_fn)
            give(fn(lc[:, :], cum[:, :], ACT.Exp, scale=-C_DECAY), wk_fn)
            take(wk_arg)
            give(fn(bonus[:, :], bonus[:, :], ACT.Sqrt), wk_fn)
            take(wk_arg)
            give(fn(work[:, :], cum[:, :], ACT.Exp, scale=C_DECAY), wk_fn)
            take(wk_arg)
            give(fn(lc[:, :], lc[:, :], ACT.Exp, scale=-C_DECAY), wk_fn)

        def rwkv_group(g):
            j, gg_ = g // GG, g % GG
            take(wk_toks)
            give(fn(toks[:, 0:2], ps[:, 6, :].rearrange("p (s i n) -> p s i n", s=2, i=2), ACT.Copy), act_step)
            give(fn(toks[:, 2], ps[:, 7, 0:2 * P].rearrange("p (i n) -> p i n", i=2), ACT.Copy), act_step)
            give(fn(km[:, :, 0:CH].rearrange("p (h i) n -> p i h n", i=2),
                    ps[:, 7, 2 * P:4 * P].rearrange("p (i h n) -> p i h n", i=2, h=2), ACT.Copy), wk_kept_act)
            for lv in range(2):
                act.wait_ge(wk_square, 4 * g + lv + 1)
                if lv == 0:
                    give(fn(km[:, :, CH:P], four(3, CH), ACT.Copy), act_step)
                give(fn(xp[(lv + 1) % 2][:, :, :], four(0), ACT.Copy), wk_kept_act)
            for lv in range(2):
                take(wk_z)
                give(fn(xp[1][:, :, :], four(1), ACT.Copy), wk_kept_act)
                if gg_ and lv == 0:
                    output_root()
            if gg_:
                output_parts(g - 1)
            take(wk_wu)
            give(fn(wu[:, :, :], four(4), ACT.Copy, scale=-1.0), wk_kept_act)
            take(wk_parts)
            give(fn(y0[:, :, :], four(6, CH), ACT.Copy), act_step)
            give(fn(bc[:, :, :].rearrange("p i c n -> p c i n"), ps[:, 3:5, 0:2 * CH].rearrange("p c (i n) -> p c i n", i=2), ACT.Copy),
                 wk_kept_act)
            if gg_ == GG - 1:
                output_root()
                output_parts(g)

        def output_root():
            take(wk_var)
            give(fn(v4, v4, ACT.Sqrt, bias=eps64, scale=1.0 / WN), wk_root)

        def output_parts(g):
            j, gg_ = g // GG, g % GG
            take(wk_out)
            cols = slice(META + 2 * P * gg_, META + 2 * P * gg_ + 2 * P)
            give(fn(act_hi[:, 4 + j, cols], yo[:, :, :].rearrange("p i n -> p (i n)"), ACT.Copy), wk_hi)

        def rwkv():
            act.wait_ge(ret_lo, NT)
            act.dma_start(rw_masks[:, :, :], t["rw_masks"]).then_inc(wk_pre, 16)
            act.dma_start(wa[:, :], t["rw"][12]).then_inc(wk_pre, 16)
            act.dma_start(sgd[:, :], t["rw"][13]).then_inc(wk_pre, 16)
            act.wait_ge(wk_pre, 48)
            give(fn(wa[0:CH, :], wa[0:CH, :], ACT.Tanh), act_step)
            give(fn(sgd[:, :], sgd[:, :], ACT.Sigmoid), wk_lora_in)
            for g in range(4 * GG):
                if g % GG == 0:
                    rwkv_pair(g // GG)
                rwkv_group(g)

        def last_product():
            act.wait_ge(act_ready, CLOSED[5])
            act.dma_start(p_raw[:, :, :], t["p_turned"]).then_inc(p_landed, 16)
            act.wait_ge(p_landed, 16)
            give(fn(p_parts[0][:, :, :], p_raw[:, :, :], ACT.Copy), p_hi_made)
            for half in range(2):
                token_sums(H_PLE + 2 * half, U_PLE + 5 * half + 3, lambda i: acc[:, i, BANK * half:BANK * half + BANK], ACT.Sigmoid)

        load_consts()
        residual(0)
        first_projection()
        attention()
        attention_norm()
        ssm_tables()
        ssm_outputs()
        glu()
        token_sums(H_MIX1, U_OUT + 3, lambda i: acc[:, i, 0:BANK])
        token_sums(H_MIX1 + 1, U_OUT + 7, lambda i: acc[:, i, BANK:D])
        residual(1)
        feed_forward(0, U_FF1)
        residual(2)
        rw_projection()
        retention()
        rwkv()
        token_sums(H_WO, U_WO + 3, lambda i: acc[:, i, 0:BANK])
        token_sums(H_WO + 1, U_WO + 7, lambda i: acc[:, i, BANK:D])
        residual(3)
        feed_forward(1, U_FF2)
        residual(4)
        last_product()
        act.wait_ge(ple_done, 2 * NT)
        residual(5)

    @block.tensor
    def _(pe):
        tally = Tally(pe)
        post, take = tally.post, tally.take

        def use_unit(u):
            pe.wait_ge(w_ready, u + 1)

        def turn_rows(c):
            if c == 0:
                pe.wait_ge(const_landed, 16 * 5)
            for g, rows, _, _ in tiles_of(c):
                pe.wait_ge(xn_ready, g + 1)
                if g >= 2:
                    pe.wait_ge(act_ready, g - 1)
                for k in range(KT):
                    if rows == META:
                        out = ps[:, 0, META * k:META * k + META]
                    else:
                        out = ps[:, 2 * (g % 2) + k // 4, P * (k % 4):P * (k % 4) + P]
                    mm = pe.transpose(out, xn[0:rows, g % 2, P * k:P * k + P], ident[0:rows, 0:rows])
                post(mm, turned)

        def feature_product(u, banks, spans):
            use_unit(u)
            for k in range(KT):
                for w, a in PASSES:
                    first, last = (k, w, a) == (0, 0, 0), (k, w, a) == (KT - 1, 1, 0)
                    for bank, (c0, c1) in zip(banks, spans):
                        mm = pe.matmul(ps[:, bank, 0:c1 - c0], ws[w][:, u % SLOTS, P * k:P * k + P], acts[a][:, k, c0:c1],
                                       start=first, stop=last)
            mm.then_inc(unit_done, 1)

        def first_projection():
            for m in range(4):
                if m >= 2:
                    pe.wait_ge(u_evac, 3 * (m - 1))
                feature_product(U_SSM + m, SPAN_BANKS[m % 2], SPANS)
            for uu in range(4):
                use_unit(U_V + uu)
            for i in range(NT + 1):
                if i >= 2:
                    pe.wait_ge(v_ready, i - 1)
                rows, c0 = (META, 0) if i == NT else (P, META + P * i)
                for k in range(KT):
                    s = (U_V + k // 2) % SLOTS
                    for w, a in PASSES:
                        mm = pe.matmul(ps[0:rows, 6 + i % 2, :], acts[a][:, k, c0:c0 + rows],
                                       ws[w][:, s, BANK * (k % 2):BANK * (k % 2) + BANK],
                                       start=(k, w, a) == (0, 0, 0), stop=(k, w, a) == (KT - 1, 1, 0))
                    if i == NT and k % 2:
                        mm.then_inc(unit_done, 1)
                if i < NT:
                    post(mm, v_psum)
            pe.wait_ge(u_evac, 12)
            groups = 0
            for m in range(9):
                if m < 8:
                    if m >= 2:
                        pe.wait_ge(qk_raw_ready, ROPE_GROUPS[m - 2])
                    n = 2 + (m >= 4)
                    feature_product(U_QK + m, SPAN_BANKS[m % 2][:n], SPANS[:n])
                if m >= 1:
                    pe.wait_ge(qk_raw_ready, ROPE_GROUPS[m - 1])
                    if m == 1:
                        pe.wait_ge(v_ready, NT + 1)
                    for c0, c1 in SPANS[:2 + (m - 1 >= 4)]:
                        if groups >= 2:
                            pe.wait_ge(rope_done, groups - 1)
                        mm = pe.matmul(ps[:, 6 + groups % 2, 0:c1 - c0], rot[:, :], qk_raw[:, (m - 1) % 2, c0:c1],
                                       start=True, stop=True)
                        post(mm, rot_psum)
                        groups += 1

        def scores(unit):
            qi, h = unit // HEADS, unit % HEADS
            p0, n = QK * (h % 2), (qi + 1) * P
            for br in range(2):
                if unit:
                    pe.wait_ge(s_exp, 2 * unit - 1 + br)
                out = score_rows(qi, br, n + META)
                q = qk_t[p0:p0 + QK, 2 * br + h // 2, META + P * qi:META + P * qi + P]
                k = qk_t[p0:p0 + QK, 4 + 2 * br + h // 2, :]
                for c in range(0, n, BANK):
                    w = min(BANK, n - c)
                    mm = pe.matmul(out[:, c:c + w], q, k[:, META + c:META + c + w], start=True, stop=True)
                pe.matmul(out[:, n - P:n], causal[:, 0, :], causal[:, 1, :], start=False, stop=True, skip_group_check=True)
                mm = pe.matmul(out[:, n:n + META], q, k[:, 0:META], start=True, stop=True, skip_group_check=True)
                post(mm, s_psum)

        def weigh_values(unit):
            qi, h = unit // HEADS, unit % HEADS
            n = (qi + 1) * P
            pe.wait_ge(a_ready, unit + 1)
            for b, (k0, nk) in enumerate(key_batches(qi)):
                turn = TURNS[unit] + b
                if turn >= 2:
                    pe.wait_ge(at_ready, turn if unit >= WIDE else turn - 1)
                bank = turn_bank(unit, turn)
                if k0 == NT:
                    mm = pe.transpose(ps[0:META, bank, 0:P], e_br[:, unit % 2, 0, n:n + META], ident[:, :])
                else:
                    for k in range(nk):
                        mm = pe.transpose(ps[:, bank, P * k:P * k + P], e_br[:, unit % 2, 0, P * (k0 + k):P * (k0 + k) + P], ident[:, :])
                post(mm, at_psum)
            pe.wait_ge(at_ready, TURNS[unit + 1])
            if unit >= 2:
                pe.wait_ge(o_ready, unit if unit >= WIDE else unit - 1)
            out = ps[:, output_bank(unit), 0:VD]
            for k in range(qi + 1):
                pe.matmul(out, a_t[:, k], v_tok[:, k, h * VD:(h + 1) * VD], start=k == 0, stop=False)
            mm = pe.matmul(out, a_t[0:META, NT], v_tok[0:META, NT, h * VD:(h + 1) * VD], start=False, stop=True)
            post(mm, o_psum)

        def attention():
            pe.wait_ge(rope_done, ROPE_GROUPS[7])
            pe.wait_ge(qk_raw_ready, ROPE_GROUPS[7])
            for unit in range(NT * HEADS):
                if unit == WIDE:
                    weigh_values(unit - 1)
                    pe.wait_ge(at_ready, TURNS[unit])
                    pe.wait_ge(o_ready, unit - 1)
                scores(unit)
                if unit and unit != WIDE:
                    weigh_values(unit - 1)
            weigh_values(NT * HEADS - 1)

        def turn_heads():
            for i in range(NT):
                pe.wait_ge(sub_normed, i + 1)
                if i >= 2:
                    pe.wait_ge(sub_lo, i - 1)
                for h in range(HEADS):
                    mm = pe.transpose(ps[:, i % 2, VD * h:VD * h + VD], o_n[:, i % 2, VD * h:VD * h + VD], ident[:, :])
                post(mm, sub_turned)

        def ssm_tables():
            pe.wait_ge(sub_lo, NT)
            for b in range(4):
                pe.wait_ge(ca_ready, b + 1)
                if b == 0:
                    pe.wait_ge(bb_ready, 1)
                for n in range(2):
                    if b:
                        pe.wait_ge(kd_ready, 2 * (b - 1) + n + 1)
                    for j in range(4):
                        g = GB * b + 4 * n + j
                        rows, q = slice(SN * (g % 2), SN * (g % 2) + SN), g // 2
                        for ri in range(2):
                            mm = pe.matmul(ps[0:SG, 2 * n + j % 2, 256 * (j // 2):256 * (j // 2) + 256], bb[rows, ri, q],
                                           ca[rows, ri, q % 4, 0:STEP, :].rearrange("p l h -> p (l h)"), start=ri == 0, stop=ri == 1)
                    post(mm, kd_psum)
                pe.wait_ge(g_ready, b + 1)
                for q in range(4):
                    n = 4 * b + q
                    if n >= 2:
                        pe.wait_ge(gt_ready, n - 1)
                    for half in range(2):
                        for ri in range(2):
                            mm = pe.transpose(ps[:, 4 + n % 2, P * (2 * half + ri):P * (2 * half + ri) + P],
                                              g_t[:, ri, q, OCT * half:OCT * half + OCT, :].rearrange("p s h -> p (s h)"), ident[:, :])
                    post(mm, g_turned)
                pe.wait_ge(gt_ready, 4 * b + 4)
                if b:
                    pe.wait_ge(ssm_x, b)
                for ri in range(2):
                    for q in range(4):
                        for par in range(2):
                            rows = slice(SN * par, SN * par + SN)
                            for half in range(2):
                                mm = pe.matmul(ps[rows, 6 + ri, NSTEP * q:NSTEP * q + NSTEP], gt[:, q, half, ri, rows],
                                               u_in[:, GB * b + 2 * q + par, half:NOCT:2], start=half == 0, stop=half == 1)
                post(mm, ssm_s)

        def ssm_outputs():
            pe.wait_ge(kd_ready, 8)
            pe.wait_ge(ssm_x, 4)
            pe.wait_ge(ssm_scanned, 1)
            for b in range(4):
                pe.wait_ge(tab_landed[b % 2], 16 * 9 * (b // 2 + 1))
                for j in range(GB):
                    g = GB * b + j
                    if g >= 8:
                        pe.wait_ge(y_gelu, g - 7)
                    rows, q = slice(SN * (g % 2), SN * (g % 2) + SN), g // 2
                    even, odd = u_in[:, g, 0:NOCT:2], u_in[:, g, 1:NOCT:2]
                    for half in range(2):
                        out = ps[:, j, NSTEP * half:NSTEP * half + NSTEP]
                        pe.matmul(out, m_t[:, b % 2, j, P * half:P * half + P], even, start=True, stop=False)
                        if half:
                            pe.matmul(out, m_t[:, b % 2, j, 0:P], odd, start=False, stop=False)
                        for ri in range(2):
                            mm = pe.matmul(out, ca2[rows, b % 2, ri, q % 4, 1 + OCT * half:1 + OCT * half + OCT, :].rearrange("p l h -> p (l h)"),
                                           xs[rows, ri, q, 0:NSTEP], start=False, stop=ri == 1)
                    post(mm, y_psum)

        def glu():
            pe.wait_ge(y_lo, 4)
            pe.wait_ge(y_gelu, GROUPS)
            for m in range(5):
                if m < 4:
                    u = U_GLU + m // 2
                    use_unit(u)
                    if m >= 2:
                        pe.wait_ge(glu_sig, m - 1)
                    for k in range(4):
                        w0 = 512 * (m % 2) + P * k
                        for w, a in PASSES:
                            for h in range(2):
                                mm = pe.matmul(ps[:, 2 * (m % 2) + h, :], ws[w][:, u % SLOTS, w0:w0 + P], (yh, yl)[a][:, k, BANK * h:BANK * h + BANK],
                                               start=(k, w, a) == (0, 0, 0), stop=(k, w, a) == (3, 1, 0))
                    mm.then_inc(unit_done, 1) if m % 2 else post(mm, glu_psum)
                if m >= 1:
                    pe.wait_ge(glu_sq, m)
                    for h in range(2):
                        mm = pe.matmul(ps[:, 4 + h, :], ones[:, :], ysq[:, (m - 1) % 2, BANK * h:BANK * h + BANK], start=m == 1, stop=m == 4)
                    post(mm, glu_sum)

        def token_half(half, units, free=None, source=acts, at=META):
            for uu, u in enumerate(units):
                use_unit(u)
                for i in range(NT):
                    if uu == 0 and free:
                        pe.wait_ge(free[0], free[1] + i + 1)
                    for kk in range(2):
                        for w, a in PASSES:
                            first, last = (uu, kk, w, a) == (0, 0, 0, 0), (uu, kk, w, a) == (len(units) - 1, 1, 1, 0)
                            mm = pe.matmul(ps[:, i, :], source[a][:, 2 * uu + kk, at + P * i:at + P * i + P], ws[w][:, u % SLOTS, BANK * kk:BANK * kk + BANK],
                                           start=first, stop=last)
                    if i == NT - 1:
                        mm.then_inc(unit_done, 1)
                    elif uu == len(units) - 1:
                        post(mm, tok_psum)

        def feed_forward(f, u0):
            def product(u, slot, bank):
                pe.wait_ge(w_ready, u + 1)
                for k in range(KT):
                    for w, a in PASSES:
                        for h in range(2):
                            mm = pe.matmul(ps[:, bank + h, :], ws[w][:, slot, P * k:P * k + P], acts[a][:, k, META + BANK * h:META + BANK * h + BANK],
                                           start=(k, w, a) == (0, 0, 0), stop=(k, w, a) == (KT - 1, 1, 0))
                mm.then_inc(unit_done, 1)

            def hidden(n, s, u):
                if not isinstance(n, int) or n >= 1:
                    pe.wait_ge(ff_silu, n + FT * f)
                product(u, s % SLOTS, 0)
                if not isinstance(n, int) or n >= 1:
                    pe.wait_ge(ff_prod, n + FT * f)
                product(u + 1, (s + 1) % SLOTS, 2)

            def down(n, par, s, u):
                pe.wait_ge(w_ready, u + 1)
                pe.wait_ge(ff_lo, n + (FT * f + 1))
                for q in range(16):
                    i, j = q // 2, q % 2
                    pe.wait_ge(down_added, n * 16 + (down_base(f) + q - 3))
                    for p_, (w, a) in enumerate(PASSES):
                        mm = pe.matmul(ps[:, 4 + q % 4, :], ffh[a][:, par, P * i:P * i + P], ws[w][:, s % SLOTS, BANK * j:BANK * j + BANK],
                                       start=p_ == 0, stop=p_ == 2)
                    mm.then_inc(down_psum if q < 15 else unit_done, 1)

            hidden(0, u0, u0)
            with pe.Fori(0, (FT - 2) // 2) as i:
                for s in range(2):
                    s0 = u0 + 2 + 3 * s
                    hidden(i * 2 + (1 + s), s0, i * 6 + s0)
                    down(i * 2 + s, s, s0 + 2, i * 6 + (s0 + 2))
            last = u0 + 2 + 3 * (FT - 2)
            hidden(FT - 1, last, last)
            down(FT - 2, 0, last + 2, last + 2)
            down(FT - 1, 1, last + 3, last + 3)

        def rw_projection():
            for m in range(RW_TILES):
                if m >= 2:
                    pe.wait_ge(rw_mixed, m - 1)
                feature_product(U_RW + m, (2 * (m % 2), 2 * (m % 2) + 1), SPANS[:2])

        def retention():
            pe.wait_ge(rw_mixed, RW_TILES)
            for j in range(4):
                token_half(H_RET + j, range(U_RET + 4 * j, U_RET + 4 * j + 4), free=(tok_done, NT * (H_RET + j - 1)) if j else None)
            pe.wait_ge(tok_done, NT * (H_RET + 4))
            pe.wait_ge(rot_done, 2 * NT)
            pe.wait_ge(ret_landed, 16 * 6)
            def front(i):
                if i:
                    pe.wait_ge(c_k, i)
                    pe.wait_ge(c_qs, i)
                for n, src in enumerate((rq, rk)):
                    for h in range(RH):
                        mm = pe.transpose(ps[:, n, P * h:P * h + P], src[:, i, RD * h:RD * h + RD], ident[:, :])
                    post(mm, c_turned)
                pe.wait_ge(c_q, i + 1)
                pe.wait_ge(c_k, i + 1)
                for h in range(RH):
                    mm = pe.matmul(ps[:, 2, P * h:P * h + P], k_t[:, h], q_t[:, h], start=True, stop=True)
                post(mm, sc_psum)

            front(0)
            for i in range(NT):
                pe.wait_ge(c_qs, i + 1)
                pe.wait_ge(sc_ready, i + 1)
                if i:
                    pe.wait_ge(ret_state, i)
                    pe.wait_ge(ret_var, i)
                for h in range(RH):
                    v = rv[:, i, RD * h:RD * h + RD]
                    mm = pe.matmul(ps[:, 3, P * h:P * h + P], s_t[:, h], v, start=True, stop=i == 0)
                    if i:
                        mm = pe.matmul(ps[:, 3, P * h:P * h + P], qs_t[:, h], r_state[:, h], start=False, stop=True)
                post(mm, ret_psum)
                pe.wait_ge(c_kend, i + 1)
                for h in range(RH):
                    mm = pe.matmul(ps[:, 4, P * h:P * h + P], k_end[:, h], rv[:, i, RD * h:RD * h + RD], start=True, stop=True)
                post(mm, ret_u)
                if i + 1 < NT:
                    front(i + 1)
                pe.wait_ge(ret_y, i + 1)
                if i:
                    pe.wait_ge(ret_lo, i)
                for h in range(RH):
                    mm = pe.transpose(ps[:, 5, P * h:P * h + P], ry[:, h], ident[:, :])
                post(mm, ret_turned)

        def rwkv_pair(j):
            if j:
                pe.wait_ge(wk_lo, GG * j)
            pe.wait_ge(wk_lora_in, 1)
            pe.wait_ge(wk_landed, 16 * 5 * (j + 1))
            for h in range(2):
                cols = slice(BANK * h, BANK * h + BANK)
                pe.matmul(ps[:, h, :], lora[0:CH, 0], wa[0:CH, cols], start=True, stop=True)
                mm = pe.matmul(ps[:, 4 + h, :], lora[:, 1], sgd[:, cols], start=True, stop=True)
            for h in range(2):
                cols = slice(BANK * h, BANK * h + BANK)
                mm = pe.matmul(ps[:, 2 + h, :], lora[CH:P, 0], wa[CH:P, cols], start=True, stop=True)
            post(mm, wk_lora)
            take(wk_sq2)
            for h in range(2):
                mm = pe.matmul(ps[:, 6 + h, :], head_ones[:, :], to_end[:, 0, BANK * h:BANK * h + BANK], start=True, stop=True)
            post(mm, wk_sums)
            take(wk_sq2)
            for h in range(2):
                mm = pe.matmul(ps[:, 6 + h, :], head_ones[:, :], to_end[:, 0, BANK * h:BANK * h + BANK], start=True, stop=True)
            post(mm, wk_sums)

        def rwkv_group(g):
            gg_ = g % GG
            t0 = 2 * P * gg_
            pe.wait_ge(wk_state, 17 * (g // GG) + 1)
            if g >= 2:
                pe.wait_ge(wk_lo, g - 1 if gg_ else g)
            head = lambda hh: slice(CH * hh, CH * hh + CH)
            for hh in range(2):
                for i in range(2):
                    tile = slice(t0 + P * i, t0 + P * i + P)
                    pair_rhs = rk_[head(hh), :, tile]
                    pe.matmul(ps[:, hh, 2 * P * i:2 * P * i + 2 * P], bh[head(hh), 0, tile], pair_rhs, start=True, stop=True)
                    mm = pe.matmul(ps[:, 4 + hh, P * i:P * i + P], rk_[head(hh), 0, tile], bh[head(hh), 0, tile], start=True, stop=True)
            post(mm, wk_mats)
            for hh in range(2):
                for i in range(2):
                    tile = slice(t0 + P * i, t0 + P * i + P)
                    mm = pe.matmul(ps[:, 2 + hh, 2 * P * i:2 * P * i + 2 * P], bh[head(hh), 1, tile], rk_[head(hh), :, tile], start=True, stop=True)
            post(mm, wk_mats)
            for i in range(2):
                tile = slice(t0 + P * i, t0 + P * i + P)
                for at, src in enumerate((to_end[:, 0, tile], to_end[:, 1, tile], vv[:, tile], rk_[:, 0, tile])):
                    c0 = 2 * P * (at % 2) + P * i
                    mm = pe.transpose(ps[:, 6 + at // 2, c0:c0 + P], src, ident[:, :])
            post(mm, wk_toks)
            take(wk_kept_dve)
            take(wk_kept_act)
            for lv in range(4):
                x, xtr = xp[lv % 2], xt[lv % 2]
                if lv:
                    take(wk_kept_dve)
                if lv in (1, 2):
                    take(wk_kept_act)
                for u in range(4):
                    out = slice(P * u, P * u + P)
                    if lv < 3:
                        mm = pe.matmul(ps[:, 1, out], x[:, u], xtr[:, u], start=True, stop=True)
                    if lv < 2:
                        mm = pe.matmul(ps[:, 0, out], xtr[:, u], x[:, u], start=True, stop=True)
                    if lv:
                        mm = pe.matmul(ps[:, 2, out], xtr[:, u], inv[:, u], start=True, stop=True)
                if lv == 0:
                    take(wk_kept_dve)
                    for u in range(4):
                        mm = pe.matmul(ps[:, 3, CH * u:CH * u + CH], k_m[:, u, 0], toks[:, 2, u % 2, head(u // 2)], start=True, stop=True)
                post(mm, wk_square)
                if gg_:
                    chunk_step(g - 1, lv)
            for lv in range(2):
                take(wk_kept_dve)
                for u in range(4):
                    pe.matmul(ps[:, 0, P * u:P * u + P], xt[0][:, u], inv[:, u], start=True, stop=True)
                    mm = pe.transpose(ps[:, 1, P * u:P * u + P], inv[:, u], ident[:, :])
                post(mm, wk_z)
                if gg_ and lv:
                    turn_outputs()
                take(wk_kept_dve)
                take(wk_kept_act)
                for u in range(4):
                    mm = pe.matmul(ps[:, 2, P * u:P * u + P], xp[1][:, u], xp[0][:, u], start=True, stop=True)
                post(mm, wk_merge)
            take(wk_kept_dve)
            pe.wait_ge(wk_lo, g)
            for u in range(4):
                mm = pe.matmul(ps[:, 4, P * u:P * u + P], inv[:, u], km[:, u], start=True, stop=True)
            post(mm, wk_wu)
            take(wk_kept_act)
            for hh in range(2):
                for i in range(2):
                    u = 2 * hh + i
                    w, uv, v = wu[:, u, 0:CH], wu[:, u, CH:P], toks[:, 2, i, head(hh)]
                    pe.matmul(ps[head(hh), 5, P * i:P * i + P], w, n_m[:, u, 1], start=True, stop=True)
                    pe.matmul(ps[:, 6, CH * u:CH * u + CH], k_m[:, u, 1], v, start=True, stop=False)
                    mm = pe.matmul(ps[:, 6, CH * u:CH * u + CH], n_m[:, u, 1], uv, start=False, stop=True)
            for c, bank in enumerate((7, 0)):
                rows = head(c)
                for hh in range(2):
                    for i in range(2):
                        u = 2 * hh + i
                        b_, k_, v = toks[rows, 0, i, head(hh)], toks[rows, 1, i, head(hh)], toks[rows, 2, i, head(hh)]
                        pe.matmul(ps[head(hh), bank, CH * i:CH * i + CH], wu[rows, u, 0:CH], b_, start=True, stop=True)
                        pe.matmul(ps[head(hh), 3 + c, CH * i:CH * i + CH], k_, v, start=True, stop=False)
                        mm = pe.matmul(ps[head(hh), 3 + c, CH * i:CH * i + CH], b_, wu[rows, u, CH:P], start=False, stop=True)
            post(mm, wk_parts)
            take(wk_kept_dve)
            take(wk_kept_act)
            if gg_ == GG - 1:
                for n in range(4):
                    chunk_step(g, n)
                turn_outputs()

        def chunk_step(g, n):
            head = lambda hh: slice(CH * hh, CH * hh + CH)
            i, c = n // 2, n % 2
            pe.wait_ge(wk_state, 17 * (g // GG) + 4 * (g % GG) + n + 1)
            for hh in range(2):
                st = state[head(hh), n % 2]
                pe.matmul(ps[head(c), 4 + hh, CH * i:CH * i + CH], rwt[head(hh), i, CH * c:CH * c + CH], st, start=True, stop=True)
                mm = pe.matmul(ps[head(hh), 6, 0:CH], ac[head(hh), i, c], st, start=True, stop=True)
            post(mm, wk_step)

        def turn_outputs():
            take(wk_kept_dve)
            for i in range(2):
                mm = pe.transpose(ps[:, 7, P * i:P * i + P], yn[:, i].rearrange("p h n -> p (h n)"), ident[:, :])
            post(mm, wk_yt)

        def rwkv():
            pe.wait_ge(ret_lo, NT)
            for g in range(4 * GG):
                if g % GG == 0:
                    rwkv_pair(g // GG)
                rwkv_group(g)

        def last_product():
            for half in range(2):
                token_half(H_PLE + 2 * half, range(U_PLE + 5 * half, U_PLE + 5 * half + 4), free=(ple_done, NT * (half - 1)) if half else None)
                pe.wait_ge(p_ready, 1)
                token_half(H_PLE + 2 * half + 1, (U_PLE + 5 * half + 4,), free=(tok_done, NT * (H_PLE + half)), source=p_parts, at=0)

        turn_rows(0)
        pe.wait_ge(act_ready, CLOSED[1])
        first_projection()
        attention()
        turn_heads()
        ssm_tables()
        ssm_outputs()
        glu()
        pe.wait_ge(glu_root, 1)
        pe.wait_ge(glu_sig, 4)
        pe.wait_ge(glu_lo, 4)
        token_half(H_MIX1, range(U_OUT, U_OUT + 4))
        token_half(H_MIX1 + 1, range(U_OUT + 4, U_OUT + 8), free=(tok_done, NT * H_MIX1))
        pe.wait_ge(tok_done, NT * (H_MIX1 + 2))
        turn_rows(1)
        pe.wait_ge(act_ready, CLOSED[2])
        feed_forward(0, U_FF1)
        pe.wait_ge(down_added, down_base(0) + 16 * FT)
        turn_rows(2)
        pe.wait_ge(act_ready, CLOSED[3])
        rw_projection()
        retention()
        rwkv()
        pe.wait_ge(wk_lo, 4 * GG)
        token_half(H_WO, range(U_WO, U_WO + 4))
        token_half(H_WO + 1, range(U_WO + 4, U_WO + 8), free=(tok_done, NT * H_WO))
        pe.wait_ge(tok_done, NT * (H_WO + 2))
        turn_rows(3)
        pe.wait_ge(act_ready, CLOSED[4])
        feed_forward(1, U_FF2)
        pe.wait_ge(down_added, down_base(1) + 16 * FT)
        turn_rows(4)
        pe.wait_ge(act_ready, CLOSED[5])
        last_product()

    @block.vector
    def _(dve):
        tally = Tally(dve)
        give, post, take = tally.give, tally.post, tally.take

        def tt(out, a, b, op, signal=dve_step):
            give(dve.tensor_tensor(out, a, b, op), signal)

        def ts(out, a, s0, op0, s1=None, op1=None, signal=dve_step):
            give(dve.tensor_scalar(out, a, s0, s1, op0) if op1 is None else dve.tensor_scalar(out, a, s0, s1, op0, op1), signal)

        def stt(out, a, s, b, op0, op1, signal=dve_step):
            give(dve.scalar_tensor_tensor(out=out, in0=a, scalar=s, in1=b, op0=op0, op1=op1), signal)

        def inverse(out, a, signal=dve_step):
            give(dve.reciprocal(out, a), signal)

        def residual(c):
            tiles = tiles_of(c)
            dve.wait_ge(gain_landed, 16 * GAINS[c])
            for step in range(len(tiles) + 2):
                if step < len(tiles) and c:
                    g = tiles[step][0]
                    if c in (1, 3):
                        dve.wait_ge(tok_done, NT * (1 + (H_MIX1 if c == 1 else H_WO)) + step + 1)
                    dve.wait_ge(row_landed[g % 3], 16 * (g // 3 + 1))
                    if post_gain[c]:
                        take(post_root)
                        r = small[:, g % 64:g % 64 + 1]
                        inverse(r, r)
                        stt(post_part[:, :], acc[:, step], r, gain_post[:, :], MUL, MUL)
                        tt(row[:, g % 3], row[:, g % 3], post_part[:, :], ADD, row_final)
                    else:
                        tt(row[:, g % 3], row[:, g % 3], acc[:, step], ADD, row_final)
                if 1 <= step <= len(tiles):
                    g, rows, _, _ = tiles[step - 1]
                    take(row_root)
                    r = small[0:rows, 64 + g % 64:65 + g % 64]
                    inverse(r, r)
                    if c == 5:
                        if step >= 3:
                            dve.wait_ge(out_stored[g % 2], 16 * ((step - 1) // 2))
                    elif g >= 2:
                        dve.wait_ge(turned, g - 1)
                    stt(xn[0:rows, g % 2], row[0:rows, g % 3], r, gain_next[0:rows, :], MUL, MUL, xn_ready)
                if step >= 2 and c < 5:
                    g, rows, _, c0 = tiles[step - 2]
                    take(hi_done)
                    if rows == META:
                        tt(act_lo[:, :, 0:META], ps[:, 0, 0:KT * META].rearrange("p (k n) -> p k n", k=KT),
                           act_hi[:, :, 0:META].bitcast(F32), SUB, act_ready)
                    else:
                        for b in range(2):
                            tt(act_lo[:, 4 * b:4 * b + 4, c0:c0 + P], ps[:, 2 * (g % 2) + b, :].rearrange("p (k n) -> p k n", k=4),
                               act_hi[:, 4 * b:4 * b + 4, c0:c0 + P].bitcast(F32), SUB, act_ready if b else dve_step)

        def first_projection():
            dve.wait_ge(rope_landed, 16)
            for m in range(8):
                for c0, c1 in SPANS[:2 + (m >= 4)]:
                    take(rot_psum)
                    g = tally.given.get(rope_done.name, 0)
                    tt(rope_sin_part[:, 0:c1 - c0], ps[:, 6 + g % 2, 0:c1 - c0], rope[:, 1, c0:c1], MUL)
                    tt(qk_t[:, m, c0:c1], qk_raw[:, m % 2, c0:c1], rope[:, 0, c0:c1], MUL)
                    tt(qk_t[:, m, c0:c1], qk_t[:, m, c0:c1], rope_sin_part[:, 0:c1 - c0], ADD, rope_done)

        def lambda_value():
            v = lam_parts[:, :].rearrange("p (b two n) -> p b two n", b=2, two=2)
            tt(v[:, :, 0], v[:, :, 0], v[:, :, 1], MUL)
            give(dve.tensor_reduce(small[:, 128:130], v[:, :, 0], X_AXIS, ADD), lam_sums)
            take(lam_exp)
            stt(small[:, 132:133], small[:, 130:131], LAM_INIT, small[:, 131:132], ADD, SUB)

        def row_maximum(unit):
            qi = unit // HEADS
            n = (qi + 1) * P + META
            for br in range(2):
                take(s_psum)
                col = 140 + 4 * (unit % 2) + br
                give(dve.tensor_reduce(small[:, col:col + 1], score_rows(qi, br, n), X_AXIS, ALU.max, negate=True), s_max)

        def difference(unit):
            n = (unit // HEADS + 1) * P + META
            z = 142 + 4 * (unit % 2)
            take(s_exp, 2)
            inverse(small[:, z:z + 2], small[:, z:z + 2])
            tt(small[:, z + 1:z + 2], small[:, z + 1:z + 2], small[:, 132:133], MUL)
            ts(e_br[:, unit % 2, 1, 0:n], e_br[:, unit % 2, 1, 0:n], small[:, z + 1:z + 2], MUL)
            stt(e_br[:, unit % 2, 0, 0:n], e_br[:, unit % 2, 0, 0:n], small[:, z:z + 1], e_br[:, unit % 2, 1, 0:n], MUL, SUB, a_ready)

        def keep_turned(unit):
            if unit:
                dve.wait_ge(o_psum, unit)
            for b, (k0, nk) in enumerate(key_batches(unit // HEADS)):
                take(at_psum)
                bank = turn_bank(unit, TURNS[unit] + b)
                rows = META if k0 == NT else P
                give(dve.tensor_copy(a_t[0:rows, k0:k0 + nk].rearrange("p k n -> p (k n)"), ps[0:rows, bank, 0:P * nk]), at_ready)

        def attention():
            lambda_value()
            for unit in range(NT * HEADS):
                if unit == WIDE:
                    keep_turned(unit - 1)
                row_maximum(unit)
                if unit and unit != WIDE:
                    keep_turned(unit - 1)
                difference(unit)
            keep_turned(NT * HEADS - 1)

        def attention_norm():
            dve.wait_ge(o_landed, 32)
            stat = lambda i: small[:, 160 + 4 * i:164 + 4 * i]
            for i in range(NT):
                tt(o_sq[:, :], o_all[:, i], o_all[:, i], MUL)
                give(dve.tensor_reduce(stat(i), o_sq[:, :].rearrange("p (h n) -> p h n", h=HEADS), X_AXIS, ADD),
                     sub_ms if i == NT - 1 else dve_step)
            take(sub_root)
            inverse(small[:, 160:192], small[:, 160:192])
            for i in range(NT + 1):
                if i < NT:
                    if i >= 2:
                        dve.wait_ge(sub_turned, i - 1)
                    o = o_n[:, i % 2].rearrange("p (h n) -> p h n", h=HEADS)
                    tt(o, o_all[:, i].rearrange("p (h n) -> p h n", h=HEADS), stat(i).unsqueeze(2).to_broadcast([P, HEADS, VD]), MUL)
                    stt(o, o, 1.0 - LAM_INIT, sub_gain[:, :].unsqueeze(1).to_broadcast([P, HEADS, VD]), MUL, MUL, sub_normed)
                if i >= 1:
                    take(sub_hi)
                    c0 = META + P * (i - 1)
                    tt(act_lo[:, 0:4, c0:c0 + P], ps[:, (i - 1) % 2, :].rearrange("p (k n) -> p k n", k=4),
                       act_hi[:, 0:4, c0:c0 + P].bitcast(F32), SUB, sub_lo)

        def cmul(out_re, out_im, ar, ai, br, bi, s, t_, negate_im=False, last=dve_step):
            tt(s, ar, br, MUL)
            tt(t_, ai, bi, MUL)
            tt(out_re, s, t_, SUB)
            tt(s, ar, bi, MUL)
            tt(t_, ai, br, MUL)
            if negate_im:
                if len(s.shape) > 3:
                    tt(s, s, t_, ADD)
                    ts(out_im, s, -1.0, MUL, signal=last)
                else:
                    stt(out_im, s, -1.0, t_, MUL, SUB, last)
            else:
                tt(out_im, s, t_, ADD, last)

        def discretise():
            w = lambda n: wv[:, n]
            are, aim = ssm_vec[:, 0], ssm_vec[:, 1]
            dve.wait_ge(ssm_landed, 16 * 13)
            take(ssm_fn)
            tt(w(1), are, w(0), MUL)
            tt(w(2), aim, w(0), MUL)
            magic, turn = 12582912.0, 2.0 * math.pi
            c1 = 6.28125
            c2 = math.floor((turn - c1) * 2.0 ** 21) / 2.0 ** 21
            c3 = turn - c1 - c2
            ts(w(5), w(2), 1.0 / turn, MUL, magic, ADD)
            ts(w(5), w(5), magic, SUB)
            stt(w(3), w(5), -c1, w(2), MUL, ADD)
            stt(w(3), w(5), -c2, w(3), MUL, ADD)
            stt(w(3), w(5), -c3, w(3), MUL, ADD)
            limit = 3.1415925
            ts(w(3), w(3), limit, ALU.min, -limit, ALU.max)
            ts(w(4), w(3), math.pi / 2, ADD)
            ts(w(6), w(4), math.pi, ALU.is_gt, -turn, MUL)
            tt(w(4), w(4), w(6), ADD)
            ts(w(4), w(4), limit, ALU.min, -limit, ALU.max, signal=ssm_arg)
            take(ssm_fn, 2)
            tt(pw[:, 0, :, 1], w(1), w(4), MUL)
            tt(pw[:, 1, :, 1], w(1), w(3), MUL)
            ar, ai = pw[:, 0, :, 1], pw[:, 1, :, 1]
            ts(w(7), ar, -1.0, ADD)
            tt(w(8), are, are, MUL)
            tt(w(9), aim, aim, MUL)
            tt(w(8), w(8), w(9), ADD)
            inverse(w(8), w(8))
            tt(w(9), w(7), are, MUL)
            tt(w(10), ai, aim, MUL)
            tt(w(9), w(9), w(10), ADD)
            tt(w(9), w(9), w(8), MUL)
            tt(w(10), ai, are, MUL)
            tt(w(11), w(7), aim, MUL)
            tt(w(10), w(10), w(11), SUB)
            tt(w(10), w(10), w(8), MUL)
            wide = lambda v, n: v.unsqueeze(2).to_broadcast([P, PAIRS, n])
            tmp = cab[:, :, 0:PAIRS * SG].rearrange("p a (q h) -> p a q h", h=SG)
            cmul(bb[:, 0], bb[:, 1], wide(w(9), SG), wide(w(10), SG), b_t[:, 0], b_t[:, 1], tmp[:, 0], tmp[:, 1], last=bb_ready)
            give(dve.memset(pw[:, 0, :, 0], 1.0), dve_step)
            give(dve.memset(pw[:, 1, :, 0], 0.0), dve_step)
            for n in (1, 2, 4, 8):
                tmp = cab[:, :, 0:PAIRS * n].rearrange("p a (q h) -> p a q h", h=n)
                cmul(pw[:, 0, :, n + 1:2 * n + 1], pw[:, 1, :, n + 1:2 * n + 1], wide(pw[:, 0, :, n], n), wide(pw[:, 1, :, n], n),
                     pw[:, 0, :, 1:n + 1], pw[:, 1, :, 1:n + 1], tmp[:, 0], tmp[:, 1])
            for ri in range(2):
                give(dve.tensor_copy(a16[:, 0, ri], pw[:, 0, :, STEP]), dve_step)
            ts(a16[:, 1, 0], pw[:, 1, :, STEP], -1.0, MUL)
            give(dve.tensor_copy(a16[:, 1, 1], pw[:, 1, :, STEP]), dve_step)
            give(dve.memset(kd[:, :, 0:P], 0.0), dve_step)
            give(dve.memset(xs[:, :, :, 0:1], 0.0), dve_step)

        def ssm_tables():
            discretise()
            for b in range(4):
                q = slice(4 * b, 4 * b + 4)
                if b:
                    dve.wait_ge(ca_stored, 16 * b)
                    dve.wait_ge(kd_psum, 2 * b)
                lags = lambda ri: pw[:, ri, q, :].unsqueeze(3).to_broadcast([P, 4, LAGS, SG])
                chan = lambda ri: c_t[:, ri, q, :].unsqueeze(2).to_broadcast([P, 4, LAGS, SG])
                tmp = cab[:, :, :].rearrange("p a (q l h) -> p a q l h", q=4, l=LAGS)
                cmul(ca[:, 0], ca[:, 1], lags(0), lags(1), chan(0), chan(1), tmp[:, 0], tmp[:, 1], negate_im=True, last=ca_ready)
                if b:
                    dve.wait_ge(g_turned, 4 * b)
                back = lambda ri: pw[:, ri, q, 0:STEP][:, :, ::-1].unsqueeze(3).to_broadcast([P, 4, STEP, SG])
                inp = lambda ri: bb[:, ri, q, :].unsqueeze(2).to_broadcast([P, 4, STEP, SG])
                tmp = cab[:, :, 0:4 * STEP * SG].rearrange("p a (q l h) -> p a q l h", q=4, l=STEP)
                cmul(g_t[:, 0], g_t[:, 1], back(0), back(1), inp(0), inp(1), tmp[:, 0], tmp[:, 1], last=g_ready)
                for n in range(2):
                    take(kd_psum)
                    if b or n:
                        dve.wait_ge(kd_stored, 16 * (2 * b + n))
                    for j in range(2):
                        give(dve.tensor_copy(kd[:, j:4:2, P:], ps[0:SG, 2 * n + j, :].rearrange("p (g n) -> p g n", g=2)), dve_step)
                    g0 = GB * b + 4 * n
                    tt(kd[:, :, P:P + SG], kd[:, :, P:P + SG], d_t[:, g0:g0 + 4, :], ADD, kd_ready)
                for n in range(4):
                    take(g_turned)
                    give(dve.tensor_copy(gt[:, n].rearrange("p a b n -> p (a b n)"), ps[:, 4 + n % 2, :]), gt_ready)
                take(ssm_s)
                for ri in range(2):
                    give(dve.tensor_copy(xs[:, ri, q, 1:NSTEP + 1], ps[:, 6 + ri, 0:4 * NSTEP].rearrange("p (q c) -> p q c", q=4)),
                         ssm_x if ri else dve_step)

        def ssm_scan():
            now = wv[:, 0:2, :]
            other = wv[:, 2:4, :]
            base = tally.given[dve_step.name]
            steps = NSTEP - 2
            def advance(c, n):
                x = xs[:, :, :, c]
                def own(ins, k):
                    ins.then_inc(dve_step, 1)
                    dve.wait_ge(dve_step, n * 4 + (base + k))
                own(dve.tensor_tensor(now, x, a16[:, 0], MUL), 1)
                own(dve.tensor_tensor(other, xs[:, ::-1, :, c], a16[:, 1], MUL), 2)
                own(dve.tensor_tensor(now, now, other, ADD), 3)
                own(dve.tensor_tensor(xs[:, :, :, c + 1], xs[:, :, :, c + 1], now, ADD), 4)
            for c in range(1, NSTEP):
                advance(c, c - 1)
            tally.given[dve_step.name] += 4 * (NSTEP - 1)
            give(dve.tensor_copy(now, now), ssm_scanned)

        def glu():
            for m in range(4):
                take(y_hi)
                tt(yl[:, m], y_raw[:, m].rearrange("p t c -> p (t c)"), yh[:, m].bitcast(F32), SUB, y_lo)
            for m in range(4):
                take(glu_sig)
                y = y_raw[:, m].rearrange("p t c -> p (t c)")
                tt(y, y, sig[:, m % 2], MUL, glu_prod)
                if m >= 2:
                    dve.wait_ge(glu_sum, m - 1)
                tt(ysq[:, m % 2], y, y, MUL, glu_sq)
            take(glu_root)
            inverse(rinv[:, :], rinv[:, :])
            for m in range(4):
                y = y_raw[:, m].rearrange("p t c -> p (t c)")
                stt(y, y, glu_vec[:, 4 + m:5 + m], rinv[:, :], MUL, MUL, glu_prod)
            for m in range(4):
                take(glu_hi)
                turned = lambda a: a[:, 4 + m, META:L].rearrange("p (c t) -> p t c", t=OCT)
                tt(turned(act_lo), y_raw[:, m], turned(act_hi).bitcast(F32), SUB, glu_lo)

        def feed_forward(f, u0):
            g0, p0, l0 = FT * f, down_base(f), 15 * FT * f
            for i in range(0, NT, 2):
                give(dve.memset(acc[:, i:i + 2, :], 0.0), down_added)

            def hidden(n, slot, up_unit):
                dve.wait_ge(ff_silu, n + (g0 + 1))
                dve.wait_ge(unit_done, up_unit + 1)
                dve.tensor_tensor(ff_f[:, slot], ff_f[:, slot], ps[:, 2:4, :].rearrange("p b n -> p (b n)"), MUL).then_inc(ff_prod, 1)
                dve.wait_ge(ff_hi, n + (g0 + 1))
                dve.tensor_tensor(ffh[1][:, slot], ff_f[:, slot], ffh[0][:, slot].bitcast(F32), SUB).then_inc(ff_lo, 1)

            def sums(n, down_unit):
                for q in range(16):
                    i, j = q // 2, q % 2
                    if q < 15:
                        dve.wait_ge(down_psum, n * 15 + (l0 + q + 1))
                    else:
                        dve.wait_ge(unit_done, down_unit + 1)
                    a = acc[:, i, BANK * j:BANK * j + BANK]
                    if q == 0:
                        dve.wait_ge(down_added, n * 16 + p0)
                    dve.tensor_tensor(a, a, ps[:, 4 + q % 4, :], ADD).then_inc(down_added, 1)

            hidden(0, 0, u0 + 1)
            with dve.Fori(0, (FT - 2) // 2) as i:
                for s in range(2):
                    u = u0 + 2 + 3 * s
                    sums(i * 2 + s, i * 6 + (u + 2))
                    hidden(i * 2 + (1 + s), (1 + s) % 2, i * 6 + (u + 1))
            last = u0 + 2 + 3 * (FT - 2)
            sums(FT - 2, last + 2)
            hidden(FT - 1, 1, last + 1)
            sums(FT - 1, last + 3)
            dve.wait_ge(down_added, p0 + 16 * FT)

        def rw_projection():
            dve.wait_ge(rw_consts, 32)
            ts(rw_vec[:, 56:60], rw_vec[:, 26:30], -1.0, MUL, 1.0, ADD)
            ts(rw_vec[:, 42:56], rw_vec[:, 0:14], -1.0, MUL, 1.0, ADD, signal=rw_one)
            for m in range(RW_TILES):
                take(rw_evac)
                flat = ps[:, 2 * (m % 2):2 * (m % 2) + 2, :].rearrange("p b n -> p (b n)")
                stt(rw_t[:, m % 2, 1:T], flat[:, 0:T - 1], rw_vec[:, m:m + 1], rw_t[:, m % 2, 1:T], MUL, ADD, rw_mixed)

        def retention():
            dve.wait_ge(ret_landed, 16 * 6)
            give(dve.memset(eps5, 1e-5), dve_step)
            part = q_t[:, :, :].rearrange("p h (n two) -> p h n two", two=2)
            for n, x in enumerate((rq, rk)):
                for i in range(NT):
                    dve.wait_ge(tok_done, NT * (H_RET + n) + i + 1)
                    v = x[:, i].rearrange("p (h n two) -> p h n two", h=RH, two=2)
                    for h in range(RH):
                        tt(part[:, h], v[:, h][:, :, ::-1], ret_sin[:, i], MUL)
                    for h in range(RH):
                        tt(v[:, h], v[:, h], ret_cos[:, i].unsqueeze(2).to_broadcast([P, RD // 2, 2]), MUL)
                    tt(v, v, part, ADD, rot_done)
            def front(i):
                dve.wait_ge(c_turned, 2 * i + 1)
                dve.wait_ge(c_q, i + 1)
                if i:
                    dve.wait_ge(ret_u, i)
                tt(qs_t[:, :, :], ps[:, 0, :].rearrange("p (h n) -> p h n", h=RH), ret_start[:, :, :], MUL, c_qs)
                tt(k_end[:, :, :], rk[:, i].rearrange("p (h n) -> p h n", h=RH), ret_end.unsqueeze(2).to_broadcast([P, RH, RD]), MUL, c_kend)
                take(sc_psum)
                tt(s_t[:, :, :], ps[:, 2, :].rearrange("p (h n) -> p h n", h=RH), ret_decay[:, :, :], MUL, sc_ready)

            front(0)
            for i in range(NT):
                if i + 1 < NT:
                    front(i + 1)
                take(ret_psum)
                y_ps = ps[:, 3, :].rearrange("p (h n) -> p h n", h=RH)
                stat = small[:, 208:212]
                var = small[:, 204:208]
                if i:
                    dve.wait_ge(ret_turned, i)
                give(dve.tensor_reduce(stat, y_ps, X_AXIS, ADD), dve_step)
                ts(stat, stat, -1.0 / RD, MUL)
                tt(ry[:, :, :], y_ps, stat.unsqueeze(2).to_broadcast([P, RH, RD]), ADD)
                sq = rq[:, i].rearrange("p (h n) -> p h n", h=RH)
                tt(sq, ry[:, :, :], ry[:, :, :], MUL)
                give(dve.tensor_reduce(var, sq, X_AXIS, ADD), ret_var)
                take(ret_u)
                u_ps = ps[:, 4, :].rearrange("p (h n) -> p h n", h=RH)
                if i == 0:
                    give(dve.tensor_copy(r_state[:, :, :], u_ps), ret_state)
                else:
                    for h in range(RH):
                        stt(r_state[:, h], r_state[:, h], GAMMA[h] ** P, u_ps[:, h], MUL, ADD, ret_state if h == RH - 1 else dve_step)
                take(ret_root)
                inverse(var, var)
                tt(ry[:, :, :], ry[:, :, :], var.unsqueeze(2).to_broadcast([P, RH, RD]), MUL)
                flat = ry[:, :, :].rearrange("p h n -> p (h n)")
                tt(flat, flat, ret_norm[:, :], MUL)
                dve.wait_ge(g_landed, 16 * (i + 1))
                tt(flat, flat, rg_in[:, :], MUL, ret_y)
                take(ret_hi)
                tt(act_lo[:, 0:4, tok_cols(i)], ps[:, 5, :].rearrange("p (k n) -> p k n", k=4), act_hi[:, 0:4, tok_cols(i)].bitcast(F32), SUB, ret_lo)

        def rwkv_pair(j):
            col = lambda n: rw_vec[:, n + j:n + j + 1]
            dve.wait_ge(wk_landed, 16 * 5 * (j + 1))
            ts(rk_[:, 0], kraw[:, :], col(22), MUL)
            tt(to_end[:, 0], rk_[:, 0], rk_[:, 0], MUL, wk_sq2)
            give(dve.memset(run[:, :], 1.0), dve_step)
            give(dve.memset(run[:, :].rearrange("p (c n) -> p c n", n=CH)[:, :, 0:1], 0.0), dve_step)
            take(wk_fn, 3)
            give(dve.tensor_tensor_scan(cum[:, :], run[:, :], lc[:, :], 0.0, MUL, ADD), dve_step)
            tt(work[:, :], cum[:, :], lc[:, :], SUB, wk_arg)
            take(wk_sums)
            ts(bonus[:, :], both(6), 1e-24, ALU.max, signal=wk_arg)
            ts(to_end[:, 1], aa[:, :], col(26), MUL, col(56), ADD)
            tt(kraw[:, :], kraw[:, :], to_end[:, 1], MUL)
            stt(to_end[:, 0], rk_[:, 1], col(30), kraw[:, :], MUL, MUL, wk_sq2)
            take(wk_fn, 3)
            inverse(bonus[:, :], bonus[:, :])
            tt(rk_[:, 0], rk_[:, 0], bonus[:, :], MUL)
            tt(aa[:, :], rk_[:, 0], aa[:, :], MUL)
            take(wk_sums)
            tt(bonus[:, :], both(6), vv[:, :], MUL)
            tt(rk_[:, 0], rk_[:, 0], work[:, :], MUL, wk_arg)
            tt(rk_[:, 1], rk_[:, 1], lc[:, :], MUL)
            give(dve.tensor_copy(chunk_decay, lc[:, CH - 1::CH]), dve_step)
            chunked = lambda a: a.rearrange("p (c n) -> p c n", n=CH)
            tt(chunked(lc[:, :]), chunked(cum[:, :])[:, :, CH - 1:CH].to_broadcast([P, T // CH, CH]), chunked(cum[:, :]), SUB, wk_arg)
            take(wk_fn)
            tt(bh[:, 0], aa[:, :], work[:, :], MUL)
            tt(bh[:, 1], kraw[:, :], work[:, :], MUL)
            take(wk_fn)
            tt(to_end[:, 0], aa[:, :], lc[:, :], MUL)
            tt(to_end[:, 1], kraw[:, :], lc[:, :], MUL)
            give(dve.memset(state[:, 0], 0.0), wk_state)

        def rwkv_group(g):
            j, gg_ = g // GG, g % GG
            take(wk_mats)
            across = lambda m, n: m.to_broadcast([P, n, P])
            for hh in range(2):
                pairs = lambda bank: ps[:, bank + hh, :].rearrange("p (i s n) -> p i s n", i=2, s=2)
                tt(n_m[:, 2 * hh:2 * hh + 2], pairs(0), rw_masks[:, 0:2].unsqueeze(1).to_broadcast([P, 2, 2, P]), MUL)
                tt(n_t[:, 2 * hh:2 * hh + 2], ps[:, 4 + hh, 0:2 * P].rearrange("p (i n) -> p i n", i=2), across(rw_masks[:, 3:4], 2), MUL)
            tt(xp[0][:, :, :], n_m[:, :, 0], across(rw_masks[:, 4:5], 4), MUL)
            tt(xt[0][:, :, :], n_t[:, :, :], across(rw_masks[:, 4:5], 4), MUL)
            tt(inv[:, :, :], xp[0][:, :, :], across(ident[:, :].unsqueeze(1), 4), ADD, wk_kept_dve)
            take(wk_mats)
            for hh in range(2):
                tt(k_m[:, 2 * hh:2 * hh + 2], ps[:, 2 + hh, :].rearrange("p (i s n) -> p i s n", i=2, s=2),
                   rw_masks[:, 1:3][:, ::-1].unsqueeze(1).to_broadcast([P, 2, 2, P]), MUL, wk_kept_dve if hh else dve_step)
            for lv in range(4):
                take(wk_square)
                if lv:
                    tt(inv[:, :, :], inv[:, :, :], four(2), ADD)
                if lv < 3:
                    give(dve.tensor_copy(xt[(lv + 1) % 2][:, :, :], four(1)), wk_kept_dve)
                if gg_:
                    next_state(lv)
            for lv in range(2):
                tt(xt[0][:, :, :], n_t[:, :, :], across(rw_masks[:, 5 + lv:6 + lv], 4), MUL, wk_kept_dve)
                if gg_ and lv:
                    output_norm()
                take(wk_z)
                give(dve.tensor_copy(xp[0][:, :, :], four(0)), wk_kept_dve)
                take(wk_merge)
                tt(inv[:, :, :], inv[:, :, :], four(2), ADD, wk_kept_dve if lv else dve_step)
            if gg_:
                outputs(g - 1)
            take(wk_parts)
            tile2 = slice(2 * P * gg_, 2 * P * gg_ + 2 * P)
            tt(rwt[:, :, :].rearrange("p i n -> p (i n)"), ps[:, 5, 0:2 * P], rk_[:, 1, tile2], ADD)
            for i in range(2):
                for c, bank in enumerate((7, 0)):
                    d = chunk_decay[:, 4 * gg_ + 2 * i + c:4 * gg_ + 2 * i + c + 1]
                    stt(ac[:, i, c], id2[:, :], d, ps[:, bank, CH * i:CH * i + CH], MUL, ADD, wk_kept_dve if i and c else dve_step)
            dve.wait_ge(wk_kept_act, 7 * (g + 1))
            if gg_ == GG - 1:
                for n in range(4):
                    next_state(n)
                output_norm()
                outputs(g)

        def next_state(n):
            take(wk_step)
            tt(state[:, (n + 1) % 2], ps[:, 6, 0:CH], bc[:, n // 2, n % 2], ADD, wk_state)

        def output_norm():
            y = y0[:, :, :]
            for hh in range(2):
                tt(y[:, 2 * hh:2 * hh + 2], y[:, 2 * hh:2 * hh + 2], ps[:, 4 + hh, 0:P].rearrange("p (i n) -> p i n", i=2), ADD)
            give(dve.tensor_reduce(m4, y, X_AXIS, ADD), dve_step)
            ts(m4, m4, -1.0 / WN, MUL)
            tt(y, y, m4.unsqueeze(2).to_broadcast([P, 4, CH]), ADD)
            turned_y = yn[:, :, :, :].rearrange("p i h n -> p h i n")
            split_y = y.rearrange("p (h i) n -> p h i n", h=2)
            tt(turned_y, split_y, split_y, MUL)
            for hh in range(2):
                give(dve.tensor_reduce(v4[:, 2 * hh:2 * hh + 2], yn[:, :, hh], X_AXIS, ADD), wk_var if hh else dve_step)
            take(wk_root)
            inverse(v4, v4)
            for hh in range(2):
                tt(yn[:, :, hh], y[:, 2 * hh:2 * hh + 2], v4[:, 2 * hh:2 * hh + 2].unsqueeze(2).to_broadcast([P, 2, CH]), MUL,
                   wk_kept_dve if hh else dve_step)

        def outputs(g):
            j, gg_ = g // GG, g % GG
            tile2 = slice(2 * P * gg_, 2 * P * gg_ + 2 * P)
            take(wk_yt)
            out = yo[:, :, :].rearrange("p i n -> p (i n)")
            ts(out, ps[:, 7, 0:2 * P], rw_vec[:, 34 + j:35 + j], MUL, rw_vec[:, 38 + j:39 + j], ADD)
            tt(out, out, bonus[:, tile2], ADD)
            tt(out, out, gg[:, tile2], MUL, wk_out)
            take(wk_hi)
            cols = slice(META + 2 * P * gg_, META + 2 * P * gg_ + 2 * P)
            tt(act_lo[:, 4 + j, cols], out, act_hi[:, 4 + j, cols].bitcast(F32), SUB, wk_lo)

        def rwkv():
            give(dve.memset(eps64, 64e-5), dve_step)
            for h in range(2):
                give(dve.tensor_copy(id2[CH * h:CH * h + CH, :], ident[CH * h:CH * h + CH, CH * h:CH * h + CH]), dve_step)
            dve.wait_ge(wk_pre, 48)
            for g in range(4 * GG):
                if g % GG == 0:
                    rwkv_pair(g // GG)
                rwkv_group(g)

        def last_product():
            take(p_hi_made)
            tt(p_parts[1][:, :, :], p_raw[:, :, :], p_parts[0][:, :, :].bitcast(F32), SUB, p_ready)
            for half in range(2):
                for i in range(NT):
                    dve.wait_ge(tok_done, NT * (H_PLE + half) + i + 1)
                    if i < NT - 1:
                        dve.wait_ge(tok_psum, (NT - 1) * (H_PLE + 2 * half + 1) + i + 1)
                    else:
                        dve.wait_ge(unit_done, U_PLE + 5 * half + 5)
                    a = acc[:, i, BANK * half:BANK * half + BANK]
                    tt(a, a, ps[:, i, :], MUL, ple_done)

        give(dve.memset(eps_col, EPS), eps_ready)
        residual(0)
        dve.wait_ge(const_landed, 16 * 5)
        first_projection()
        attention()
        attention_norm()
        ssm_tables()
        ssm_scan()
        glu()
        residual(1)
        feed_forward(0, U_FF1)
        residual(2)
        rw_projection()
        retention()
        rwkv()
        residual(3)
        feed_forward(1, U_FF2)
        residual(4)
        last_product()
        residual(5)

    ctx.close()


def declare(nc, arrays):
    t = {k: nc.dram_tensor(k, a.shape, mybir.dt.from_np(a.dtype), kind="ExternalInput").ap() for k, a in arrays.items()}
    scratch = {"res": (T, D), "u_scratch": (4, P, OCT, NOCT), "o_scratch": (NT, P, HEADS * VD), "ca_scratch": (4, P, 2, 4, LAGS, SG), "kd_scratch": (SG, GROUPS, 24 * SG), "y_scratch": (P, GROUPS, NOCT),
               "rw": (RW_TILES, P, T), "g_scratch": (NT, P, RH * RD)}
    for k, shape in scratch.items():
        t[k] = nc.dram_tensor(k, shape, F32, kind="Internal").ap()
    t["out"] = nc.dram_tensor("out", (T, D), F32, kind="ExternalOutput").ap()
    return t


def constants():
    f = np.float32
    c = {"ident": np.eye(P, dtype=f), "ones": np.ones((P, P), f)}
    rot = np.zeros((P, P), f)
    half = ROT // 2
    for base in (0, QK):
        for d in range(half):
            rot[base + d + half, base + d] = -1.0
            rot[base + d, base + d + half] = 1.0
    c["rot"] = rot
    mask = np.where(np.arange(P)[None, :] <= np.arange(P)[:, None], 0.0, -1e30)
    c["causal"] = np.stack([np.eye(P), mask], 1).astype(mybir.dt.np(BF16))
    inv_freq = (f(THETA) ** (-np.arange(0, ROT, 2, dtype=f) / f(ROT))).astype(f)
    ang = np.arange(L, dtype=f)[:, None] * inv_freq[None, :]
    ang = np.concatenate([ang, ang], -1)
    rope = np.zeros((P, 2, L), f)
    rope[:, 0] = 1.0
    for base in (0, QK):
        rope[base:base + ROT, 0] = np.cos(ang).T
        rope[base:base + ROT, 1] = np.sin(ang).T
    c["rope"] = rope
    s, q = np.arange(P)[:, None], np.arange(P)[None, :]
    same = lambda n: (s // n) == (q // n)
    m = [same(CH) & (s < q), same(CH) & (s <= q), same(CH) & (s < q), -(same(CH) & (s > q)).astype(f), same(16),
         same(32) & (s // 16 > q // 16), same(64) & (s // 32 > q // 32)]
    m[0] = -m[0].astype(f)
    c["rw_masks"] = np.stack([a.astype(f) for a in m], 1)
    c["head_ones"] = same(WN).astype(f)
    pos = np.arange(T, dtype=f)
    angle = (1.0 / (f(10000.0) ** np.linspace(0.0, 1.0, RD // 2, dtype=f))).astype(f)
    phase = (pos[:, None] * angle[None, :]).astype(f)
    c["ret_cos"] = np.cos(phase).reshape(NT, P, RD // 2).transpose(1, 0, 2)
    sin = np.sin(phase).reshape(NT, P, RD // 2).transpose(1, 0, 2)
    c["ret_sin"] = np.stack([-sin, sin], -1)
    log_g = np.log(1.0 - 2.0 ** (-5.0 - np.arange(RH, dtype=np.float64)))
    idx = np.arange(P)
    rel = idx[None, :] - idx[:, None]
    c["ret_decay"] = np.stack([np.where(rel >= 0, np.exp(g * np.maximum(rel, 0)), 0.0) for g in log_g], 1).astype(f)
    c["ret_start"] = np.broadcast_to(np.stack([np.exp(g * (idx + 1.0)) for g in log_g])[None], (P, RH, P)).astype(f)
    c["ret_end"] = np.stack([np.exp(g * (P - 1.0 - idx)) for g in log_g], 1).astype(f)
    return c


def weight_stream(w_in, w_glu, w_out, w_gate, w_up, w_down, w_in_2, w_o_2, w_gate_2, w_up_2, w_down_2, w_ple_gate_2, w_ple_up_2):
    units = np.empty((UNITS, P, 1024), w_in.dtype)
    n = 0

    def features(w, c0):
        nonlocal n
        units[n] = w[:, c0:c0 + P].reshape(KT, P, P).transpose(1, 0, 2).reshape(P, 1024)
        n += 1

    def columns(w, c0):
        nonlocal n
        for k in range(0, w.shape[0], 2 * P):
            units[n] = w[k:k + 2 * P, c0:c0 + BANK].reshape(2, P, BANK).transpose(1, 0, 2).reshape(P, 1024)
            n += 1

    def feed_forward(gate, up, down):
        nonlocal n
        for m in range(FT):
            features(gate, P * m)
            features(up, P * m)
            if m:
                units[n] = down[P * (m - 1):P * m]
                n += 1
        units[n] = down[P * (FT - 1):]
        n += 1

    qk = 4 * HEADS * QK
    for m in range(4):
        features(w_in, qk + HEADS * VD + P * m)
    columns(w_in, qk)
    for m in range(8):
        features(w_in, P * m)
    for m in range(0, 4, 2):
        units[n] = w_glu.reshape(4, P, 4, P).transpose(1, 2, 0, 3)[:, m:m + 2].reshape(P, 1024)
        n += 1
    for c in range(0, D, BANK):
        columns(w_out, c)
    feed_forward(w_gate, w_up, w_down)
    for m in range(RW_TILES):
        features(w_in_2, 4 * RH * RD + P * m)
    for c in range(0, 4 * RH * RD, BANK):
        columns(w_in_2, c)
    for c in range(0, D, BANK):
        columns(w_o_2, c)
    feed_forward(w_gate_2, w_up_2, w_down_2)
    for c in range(0, D, BANK):
        columns(w_ple_gate_2, c)
        columns(w_ple_up_2, c)
    assert n == UNITS
    return units


def laid_out(i):
    a = constants()
    a["x"], a["meta"] = i["x"][0], i["meta"]
    a["weights"] = weight_stream(*(i[k][0] for k in (
        "w_in", "w_glu", "w_out", "w_gate", "w_up", "w_down", "w_in_2", "w_o_2", "w_gate_2", "w_up_2", "w_down_2",
        "w_ple_gate_2", "w_ple_up_2")))
    for k in ("pre_mix_g", "post_mix_g", "pre_ffn_g", "post_ffn_g", "subln_g", "norm_mix_w_2", "norm_ffn_w_2", "norm_ple_w_2"):
        a[k] = i[k][0]
    a["final_norm_w_2"] = i["final_norm_w_2"]
    lam = np.concatenate([i[k][0] for k in ("lambda_q1", "lambda_k1", "lambda_q2", "lambda_k2")])
    a["lam_vectors"] = np.broadcast_to(lam, (P, 4 * QK))
    pair = lambda v: v.reshape(PAIRS, 2, SN).transpose(1, 2, 0).reshape(P, PAIRS)
    dt = np.broadcast_to(i["log_dt"][0][:, None], (GROUPS, SN))
    a["ssm_vec"] = np.stack([pair(i["a_re"][0]), pair(i["a_im"][0]), pair(dt)], 1)
    pair_b = lambda v: v.reshape(PAIRS, 2, SN, SG).transpose(1, 2, 0, 3).reshape(P, PAIRS, SG)
    a["ssm_b"] = np.stack([pair_b(i["b_re"][0]), pair_b(i["b_im"][0])], 1)
    a["ssm_c"] = np.stack([pair_b(i["c_re"][0].transpose(0, 2, 1)), pair_b(i["c_im"][0].transpose(0, 2, 1))], 1)
    skip = np.zeros((SG, GROUPS, SG), i["d_skip"].dtype)
    for h in range(SG):
        skip[h, :, h] = i["d_skip"][0].reshape(GROUPS, SG)[:, h]
    a["ssm_d"] = skip
    column = lambda v: v.reshape(-1, P).T
    a["glu_vec"] = np.concatenate([column(i["b_glu"][0]), column(i["ssm_out_g"][0])], 1)
    a["rw_vec"] = np.concatenate([column(i[k + "_2"].reshape(-1)) for k in (
        "rw_mu", "rw_w0", "rw_a0", "rw_k_k", "rw_k_a", "rw_r_k", "rw_ln_w", "rw_ln_b")], 1)
    a["rw_w2a2"] = np.concatenate([i["rw_w2_2"][0], i["rw_a2_2"][0]], 0)
    a["rw_g2"] = i["rw_g2_2"][0]
    a["ret_norm"] = i["ret_norm_w_2"][0]
    a["p_turned"] = i["p_2"][0, 0].reshape(T, 2, P).transpose(2, 1, 0)
    return {k: np.ascontiguousarray(v) for k, v in a.items()}


def kernel(**inputs):
    import concourse.bacc as bacc
    from concourse.bass_utils import run_bass_kernel_spmd

    nc = bacc.Bacc("TRN2", target_bir_lowering=False, num_devices=1)
    arrays = laid_out({k: np.asarray(v) for k, v in inputs.items()})
    t = declare(nc, arrays)
    build(nc, t)
    r = run_bass_kernel_spmd(nc, [arrays], core_ids=[0])
    return r.results[0]["out"].reshape(1, T, D)
```
